# Optimizing a Trainium2 kernel written in Bass

```python
import jax, jax.numpy as jnp
from jax import lax
import numpy as np

D_MODEL = 1024
BATCH = 1
SEQ = 512
DEPTH = 1
DEC_BATCH = 1
DEC_SEQ = 2048
PAST_LEN = 128

GRID_W = 64
GLA_HEADS = 4
GLA_DK = 64
GLA_DV = 128
GLA_LOWRANK = 16
GLA_TAU = 16.0
GLA_CHUNK = 64
NA_HEADS = 8
NA_DH = 64
NA_WIN_R = 8
NA_WIN_C = 16
NA_QBLOCK_C = 16
NA_BAND_C = 32
MIX_W = GLA_HEADS * GLA_DV + NA_HEADS * NA_DH
D_FF = 2816
CONV_W = 3
LN_EPS = 1e-5
RMS_EPS = 1e-6
DEEPNORM_ALPHA = (2.0 * DEPTH) ** 0.25
DEEPNORM_BETA = (8.0 * DEPTH) ** -0.25
IN_SIZES = (GLA_HEADS * GLA_DK, GLA_HEADS * GLA_DK, GLA_HEADS * GLA_DV, GLA_HEADS * GLA_DV,
            2 * GLA_LOWRANK, NA_HEADS * NA_DH, NA_HEADS * NA_DH, NA_HEADS * NA_DH)
IN_W = sum(IN_SIZES)

kernel_name = 'hymba_gla_natten_deepnorm_encoder'

def _split_points(sizes):
    pts, acc = [], 0
    for s in sizes[:-1]:
        acc += s
        pts.append(acc)
    return pts

def layer_norm(x, g, b):
    xf = x.astype(jnp.float32)
    mu = jnp.mean(xf, axis=-1, keepdims=True)
    var = jnp.mean(jnp.square(xf - mu), axis=-1, keepdims=True)
    y = (xf - mu) * lax.rsqrt(var + LN_EPS) * g.astype(jnp.float32) + b.astype(jnp.float32)
    return y.astype(x.dtype)

def to_heads(t, n_heads):
    B, T, _ = t.shape
    return t.reshape(B, T, n_heads, -1).transpose(0, 2, 1, 3)

def gla_chunked(q, k, v, log_a):
    B, H, T, dk = q.shape
    dv = v.shape[-1]
    n = T // GLA_CHUNK
    q = q.reshape(B, H, n, GLA_CHUNK, dk)
    k = k.reshape(B, H, n, GLA_CHUNK, dk)
    v = v.reshape(B, H, n, GLA_CHUNK, dv)
    b = jnp.cumsum(log_a.reshape(B, H, n, GLA_CHUNK, dk), axis=3)
    b_last = b[:, :, :, -1:, :]
    q_in = q * jnp.exp(b)
    k_in = k * jnp.exp(-b)
    k_end = k * jnp.exp(b_last - b)
    lower = jnp.tril(jnp.ones((GLA_CHUNK, GLA_CHUNK), dtype=bool))
    a = jnp.where(lower, jnp.einsum('bhnid,bhnjd->bhnij', q_in, k_in), 0.0)
    o_intra = jnp.einsum('bhnij,bhnjv->bhniv', a, v)
    u = jnp.einsum('bhnjd,bhnjv->nbhdv', k_end, v)
    decay = jnp.exp(b_last[:, :, :, 0, :]).transpose(2, 0, 1, 3)

    def step(s, inp):
        d_c, u_c = inp
        return d_c[..., None] * s + u_c, s

    _, s_prev = lax.scan(step, jnp.zeros((B, H, dk, dv), q.dtype), (decay, u))
    o_inter = jnp.einsum('bhnid,nbhdv->bhniv', q_in, s_prev)
    return (o_intra + o_inter).reshape(B, H, T, dv)

def gla_mixer(q, k, v, g, lr, w_gate_fwd, b_gate_fwd, w_gate_bwd, b_gate_bwd, norm_g):
    dtype = q.dtype
    lr_f, lr_b = jnp.split(lr, 2, axis=-1)
    la_f = jax.nn.log_sigmoid((lr_f @ w_gate_fwd + b_gate_fwd).astype(jnp.float32)) / GLA_TAU
    la_b = jax.nn.log_sigmoid((lr_b @ w_gate_bwd + b_gate_bwd).astype(jnp.float32)) / GLA_TAU
    qh = to_heads(q, GLA_HEADS).astype(jnp.float32) * (GLA_DK ** -0.5)
    kh = to_heads(k, GLA_HEADS).astype(jnp.float32)
    vh = to_heads(v, GLA_HEADS).astype(jnp.float32)
    la_f = to_heads(la_f, GLA_HEADS)
    la_b = to_heads(la_b, GLA_HEADS)
    flip = lambda t: jnp.flip(t, axis=2)
    o = gla_chunked(qh, kh, vh, la_f) + flip(gla_chunked(flip(qh), flip(kh), flip(vh), flip(la_b)))
    o = o * lax.rsqrt(jnp.mean(jnp.square(o), axis=-1, keepdims=True) + RMS_EPS) * norm_g.astype(jnp.float32)
    B, H, T, dv = o.shape
    o = o.transpose(0, 2, 1, 3).reshape(B, T, H * dv).astype(dtype)
    return o * jax.nn.silu(g)

def neighbourhood_attention(q, k, v, rpb):
    B, T, _ = q.shape
    rows = T // GRID_W
    kr = min(NA_WIN_R, rows)
    ncb = GRID_W // NA_QBLOCK_C
    r = jnp.arange(rows)
    row_start = jnp.clip(r - kr // 2, 0, rows - kr)
    key_rows = row_start[:, None] + jnp.arange(kr)[None, :]
    qcols = jnp.arange(GRID_W).reshape(ncb, NA_QBLOCK_C)
    q_col_start = jnp.clip(qcols - NA_WIN_C // 2, 0, GRID_W - NA_WIN_C)
    band_start = jnp.clip(jnp.arange(ncb) * NA_QBLOCK_C - NA_WIN_C // 2, 0, GRID_W - NA_BAND_C)
    band_cols = band_start[:, None] + jnp.arange(NA_BAND_C)[None, :]
    col_in = ((band_cols[:, None, :] >= q_col_start[..., None]) &
              (band_cols[:, None, :] < q_col_start[..., None] + NA_WIN_C))
    dr = key_rows - r[:, None]
    dc = jnp.clip(band_cols[:, None, :] - qcols[..., None], -(NA_WIN_C - 1), NA_WIN_C - 1)
    bias = rpb[:, (dr + NA_WIN_R - 1)[:, None, None, :, None],
               (dc + NA_WIN_C - 1)[None, :, :, None, :]]
    qh = to_heads(q, NA_HEADS).reshape(B, NA_HEADS, rows, ncb, NA_QBLOCK_C, NA_DH)
    kh = to_heads(k, NA_HEADS).reshape(B, NA_HEADS, rows, GRID_W, NA_DH)
    vh = to_heads(v, NA_HEADS).reshape(B, NA_HEADS, rows, GRID_W, NA_DH)
    ri = key_rows[:, None, :, None]
    ci = band_cols[None, :, None, :]
    kg = kh[:, :, ri, ci]
    vg = vh[:, :, ri, ci]
    s = jnp.einsum('bhrnqd,bhrnkcd->bhrnqkc', qh, kg).astype(jnp.float32) * (NA_DH ** -0.5)
    s = s + bias.astype(jnp.float32)[None]
    s = jnp.where(col_in[None, None, None, :, :, None, :], s, -jnp.inf)
    p = jax.nn.softmax(s, axis=(-2, -1))
    o = jnp.einsum('bhrnqkc,bhrnkcd->bhrnqd', p.astype(v.dtype), vg)
    return o.reshape(B, NA_HEADS, T, NA_DH).transpose(0, 2, 1, 3).reshape(B, T, NA_HEADS * NA_DH)

def conv_gated_mlp(x, w_up, conv_w, conv_b, w_down):
    h = x @ w_up
    zero = jnp.zeros_like(h[:, :1])
    h_prev = jnp.concatenate([zero, h[:, :-1]], axis=1)
    h_next = jnp.concatenate([h[:, 1:], zero], axis=1)
    h = h_prev * conv_w[0] + h * conv_w[1] + h_next * conv_w[2] + conv_b
    a, gate = jnp.split(h, 2, axis=-1)
    return (jax.nn.silu(gate) * a) @ w_down

def encoder_trunk(x, ln_in_g, ln_in_b, w_in, gla_gate_w_fwd, gla_gate_b_fwd, gla_gate_w_bwd,
                  gla_gate_b_bwd, gla_norm_g, na_rpb, w_out, ln1_g, ln1_b, w_up, conv_w, conv_b,
                  w_down, ln2_g, ln2_b):
    x = layer_norm(x, ln_in_g, ln_in_b)
    pts = _split_points(IN_SIZES)
    for l in range(DEPTH):
        proj = x @ w_in[l]
        gq, gk, gv, gg, glr, nq, nk, nv = jnp.split(proj, pts, axis=-1)
        o_gla = gla_mixer(gq, gk, gv, gg, glr, gla_gate_w_fwd[l], gla_gate_b_fwd[l],
                          gla_gate_w_bwd[l], gla_gate_b_bwd[l], gla_norm_g[l])
        o_na = neighbourhood_attention(nq, nk, nv, na_rpb[l])
        mix = jnp.concatenate([o_gla, o_na], axis=-1) @ w_out[l]
        x = layer_norm(DEEPNORM_ALPHA * x + mix, ln1_g[l], ln1_b[l])
        f = conv_gated_mlp(x, w_up[l], conv_w[l], conv_b[l], w_down[l])
        x = layer_norm(DEEPNORM_ALPHA * x + f, ln2_g[l], ln2_b[l])
    return x

def setup_inputs(seed: int = 0) -> dict:
    key = jax.random.key(seed)
    ks = jax.random.split(key, 24)
    nrm = lambda k, shape, scale: jax.random.normal(k, shape, jnp.float32) * scale
    gain = lambda k, shape: 1.0 + 0.02 * jax.random.normal(k, shape, jnp.float32)
    return {
        'x_prompt': nrm(ks[0], (BATCH, SEQ, D_MODEL), 1.0),
        'x_sample': nrm(ks[1], (DEC_BATCH, DEC_SEQ, D_MODEL), 1.0),
        'ln_in_g': gain(ks[2], (D_MODEL,)),
        'ln_in_b': nrm(ks[3], (D_MODEL,), 0.02),
        'w_in': nrm(ks[4], (DEPTH, D_MODEL, IN_W), D_MODEL ** -0.5),
        'gla_gate_w_fwd': nrm(ks[5], (DEPTH, GLA_LOWRANK, GLA_HEADS * GLA_DK), GLA_LOWRANK ** -0.5),
        'gla_gate_b_fwd': nrm(ks[6], (DEPTH, GLA_HEADS * GLA_DK), 0.1),
        'gla_gate_w_bwd': nrm(ks[7], (DEPTH, GLA_LOWRANK, GLA_HEADS * GLA_DK), GLA_LOWRANK ** -0.5),
        'gla_gate_b_bwd': nrm(ks[8], (DEPTH, GLA_HEADS * GLA_DK), 0.1),
        'gla_norm_g': gain(ks[9], (DEPTH, GLA_DV)),
        'na_rpb': nrm(ks[10], (DEPTH, NA_HEADS, 2 * NA_WIN_R - 1, 2 * NA_WIN_C - 1), 0.1),
        'w_out': nrm(ks[11], (DEPTH, MIX_W, D_MODEL), DEEPNORM_BETA * MIX_W ** -0.5),
        'ln1_g': gain(ks[12], (DEPTH, D_MODEL)),
        'ln1_b': nrm(ks[13], (DEPTH, D_MODEL), 0.02),
        'w_up': nrm(ks[14], (DEPTH, D_MODEL, 2 * D_FF), D_MODEL ** -0.5),
        'conv_w': nrm(ks[15], (DEPTH, CONV_W, 2 * D_FF), CONV_W ** -0.5),
        'conv_b': nrm(ks[16], (DEPTH, 2 * D_FF), 0.02),
        'w_down': nrm(ks[17], (DEPTH, D_FF, D_MODEL), DEEPNORM_BETA * D_FF ** -0.5),
        'ln2_g': gain(ks[18], (DEPTH, D_MODEL)),
        'ln2_b': nrm(ks[19], (DEPTH, D_MODEL), 0.02),
    }

def reference(x_prompt, x_sample, ln_in_g, ln_in_b, w_in, gla_gate_w_fwd, gla_gate_b_fwd,
              gla_gate_w_bwd, gla_gate_b_bwd, gla_norm_g, na_rpb, w_out, ln1_g, ln1_b, w_up,
              conv_w, conv_b, w_down, ln2_g, ln2_b):
    y_prompt = encoder_trunk(x_prompt, ln_in_g, ln_in_b, w_in, gla_gate_w_fwd, gla_gate_b_fwd,
                             gla_gate_w_bwd, gla_gate_b_bwd, gla_norm_g, na_rpb, w_out, ln1_g,
                             ln1_b, w_up, conv_w, conv_b, w_down, ln2_g, ln2_b)
    y_sample = encoder_trunk(x_sample, ln_in_g, ln_in_b, w_in, gla_gate_w_fwd, gla_gate_b_fwd,
                             gla_gate_w_bwd, gla_gate_b_bwd, gla_norm_g, na_rpb, w_out, ln1_g,
                             ln1_b, w_up, conv_w, conv_b, w_down, ln2_g, ln2_b)
    return (y_prompt, y_sample)


_drawn_inputs = setup_inputs


def setup_inputs(seed=0):
    import zlib

    import numpy as np

    out = dict(_drawn_inputs(seed))
    spreads = {}
    factors = {'gla_gate_w_fwd': 3.559,
     'gla_gate_b_fwd': 8.0,
     'gla_gate_w_bwd': 3.74,
     'gla_gate_b_bwd': 8.0,
     'gla_norm_g': 8.0,
     'na_rpb': 8.0,
     'ln1_g': 2.77,
     'conv_b': 6.759,
     'ln2_g': 8.43,
     'ln2_b': 8.253,
     'ln1_b': 6.307}
    for name, (base, spread) in spreads.items():
        noise = np.random.default_rng([zlib.crc32(name.encode()), seed]).standard_normal(out[name].shape)
        drawn = base * np.exp(spread * noise) if base else spread * noise
        out[name] = __import__('jax').numpy.asarray(drawn.astype(out[name].dtype))
    for name, factor in factors.items():
        out[name] = (out[name] * factor).astype(out[name].dtype)
    return out
```

```python
from contextlib import ExitStack

import concourse.bass as bass
from concourse import mybir
import numpy as np

ALU = mybir.AluOpType
ACT = mybir.ActivationFunctionType
F32 = mybir.dt.float32
F32R = mybir.dt.float32r
I32 = mybir.dt.int32
AX_X = mybir.AxisListType.X

P = 128
D = 1024
KC = D // P
T_PROMPT, T_SAMPLE = 512, 2048
TOK = T_PROMPT + T_SAMPLE
BLK = 512
NBLK = TOK // BLK
TPB = BLK // P
NT = TOK // P

GLA_H, DK, DV, LOWRANK, TAU, CHUNK = 4, 64, 128, 16, 16.0, 64
NCHUNK = TOK // CHUNK
NA_H, DH = 8, 64
GRID_W, WIN_R, WIN_C, QB_C, BAND = 64, 8, 16, 16, 32
D_FF = 2816
FC = D_FF // P
LN_EPS, RMS_EPS = 1e-5, 1e-6
ALPHA = 2.0 ** 0.25
MASKED = -1e30
START = 1

GROUPS = 6
UNITS = 4
T_GROUPS = 3


def by_blocks(eng, n, body):
    with eng.Fori(0, n - 1) as b:
        body(b, False)
    body(n - 1, True)


def past(n):
    return START + n


def hold(eng, sem, value):
    eng.wait_ge(sem, value)
    eng.nop(nofuse=True)


def three_pass(pe, out, lhs, rhs, first, last, skip=False):
    (lh, ll), (rh, rl) = lhs, rhs
    pe.matmul(out, lh, rh, start=first, stop=False, skip_group_check=skip)
    pe.matmul(out, lh, rl, start=False, stop=False, skip_group_check=skip)
    return pe.matmul(out, ll, rh, start=False, stop=last, skip_group_check=skip)


class Store:

    def __init__(self, nc, ctx, stage):
        self.nc, self.ctx, self.stage = nc, ctx, stage
        self.sems = []

    def sb(self, name, shape, dt=F32):
        return self.ctx.enter_context(self.nc.sbuf_tensor(f"{self.stage}_{name}", shape, dt))

    def ps(self, name, shape, dt=F32):
        return self.ctx.enter_context(self.nc.psum_tensor(f"{self.stage}_{name}", shape, dt))

    def sem(self, name):
        self.sems.append(self.ctx.enter_context(self.nc.semaphore(f"{self.stage}_{name}")))
        return self.sems[-1]

    def pool_dma_sem(self, name):
        return self.ctx.enter_context(self.nc.semaphore(f"{self.stage}_{name}"))

    def start(self):
        with self.nc.Block() as block:
            @block.sync
            def _(sp):
                for sem in self.sems:
                    sp.sem_inc(sem, START)


def project(nc, x, ln_g, ln_b, w_groups, w_lr, ident_in, xln, qk_t, lr_t, tok_proj):
    with ExitStack() as ctx:
        st = Store(nc, ctx, "project")
        ident = st.sb("ident", [P, P])
        gain, shift = st.sb("gain", [P, D]), st.sb("shift", [P, D])
        xb = st.sb("xb", [P, TPB, D])
        stats = st.sb("stats", [P, TPB, 2, 6])
        agg = st.sb("agg", [P, TPB, 2])
        std, rstd = st.sb("std", [P, TPB]), st.sb("rstd", [P, TPB])
        eps = st.sb("eps", [P, 1])
        xt_hi, xt_lo = st.sb("xt_hi", [P, KC, BLK], F32R), st.sb("xt_lo", [P, KC, BLK], F32R)
        w_raw = st.sb("w_raw", [P, 2, UNITS, KC, P])
        w_hi, w_lo = (st.sb(f"w_{s}", [P, 2, UNITS, KC, P], F32R) for s in ("hi", "lo"))
        lr_raw = w_raw[:, 1, 0]
        lr_hi, lr_lo = st.sb("lr_hi", [P, KC, P], F32R), st.sb("lr_lo", [P, KC, P], F32R)
        out = st.sb("out", [P, UNITS, BLK])
        out_lr = st.sb("out_lr", [P, BLK])
        ps_t = st.ps("ps_t", [P, 2, BLK])
        ps_o = st.ps("ps_o", [P, UNITS, BLK])
        ps_lr = st.ps("ps_lr", [P, BLK])

        consts_in = st.sem("consts_in")
        x_in = st.sem("x_in")
        x_stored = st.sem("x_stored")
        w_in_slot = [st.sem(f"w_in_{i}") for i in range(2)]
        eps_set = st.sem("eps_set")
        stats_done = st.sem("stats_done")
        std_done = st.sem("std_done")
        ln_step = st.sem("ln_step")
        tr_done = st.sem("tr_done")
        xt_hi_done, xt_lo_done = st.sem("xt_hi_done"), st.sem("xt_lo_done")
        hi_done, lo_done = st.sem("hi_done"), st.sem("lo_done")
        lr_hi_done, lr_lo_done = st.sem("lr_hi_done"), st.sem("lr_lo_done")
        acc_done = st.sem("acc_done")
        lr_done = st.sem("lr_done")
        copied_act, copied_dve = st.sem("copied_act"), st.sem("copied_dve")
        lr_copied = st.sem("lr_copied")
        out_stored = [st.sem(f"out_stored_{u}") for u in range(UNITS)]
        lr_stored = st.sem("lr_stored")
        LN_STEPS = 2 + 3 * TPB
        st.start()
        block = ctx.enter_context(nc.Block())

        def x_rows(b):
            return x[bass.ds(b * BLK, BLK), :].rearrange("(t p) d -> p t d", p=P)

        @block.sync
        def _(sp):
            sp.dma_start(xb[:], x_rows(0)).then_inc(x_in, 16)
            sp.dma_start(gain[:], ln_g.partition_broadcast(P)).then_inc(consts_in, 16)
            sp.dma_start(shift[:], ln_b.partition_broadcast(P)).then_inc(consts_in, 16)
            sp.dma_start(ident[:], ident_in).then_inc(consts_in, 16)
            sp.dma_start(lr_raw, w_lr).then_inc(consts_in, 16)
            sp.dma_start(w_raw[:, 0], w_groups[0]).then_inc(w_in_slot[0], 16)
            hold(sp, lr_lo_done, past(1))

            def load(b, g, last):
                if not (last and g == GROUPS):
                    hold(sp, lo_done, past(b * GROUPS * UNITS + (g - 1) * UNITS))
                    sp.dma_start(w_raw[:, g % 2], w_groups[g % GROUPS]).then_inc(w_in_slot[g % 2], 16)

            def body(b, last):
                hold(sp, ln_step, past((b + 1) * LN_STEPS))
                sp.dma_start(xln[bass.ds(b * BLK, BLK), :].rearrange("(t p) d -> p t d", p=P),
                             xb[:]).then_inc(x_stored, 16)
                load(b, 1, last)
                if not last:
                    hold(sp, x_stored, past((b + 1) * 16))
                    hold(sp, tr_done, past((b + 1) * KC))
                    sp.dma_start(xb[:], x_rows(b + 1)).then_inc(x_in, 16)
                hold(sp, lr_copied, past(b + 1))
                sp.dma_start(lr_t[:, bass.ds(b * BLK, BLK)], out_lr[0:2 * LOWRANK, :]).then_inc(lr_stored, 16)
                for g in range(GROUPS):
                    if g:
                        load(b, g + 1, last)
                    for u in range(UNITS):
                        hold(sp, copied_act if u < 2 else copied_dve, past(b * GROUPS * 2 + g * 2 + u % 2 + 1))
                        if g < T_GROUPS:
                            dst = qk_t[(g * UNITS + u) * P:(g * UNITS + u + 1) * P, bass.ds(b * BLK, BLK)]
                        else:
                            dst = tok_proj[g - T_GROUPS, bass.ds(b * BLK + u * P, P), :]
                        sp.dma_start(dst, out[:, u, :]).then_inc(out_stored[u], 16)
            by_blocks(sp, NBLK, body)
            for sem, n in [(x_stored, NBLK), (lr_stored, NBLK)] + [(s, NBLK * GROUPS) for s in out_stored]:
                hold(sp, sem, past(16 * n))

        @block.scalar
        def _(act):
            def split_hi(n_in_block, b, g, u):
                if u == 0:
                    act.wait_ge(w_in_slot[g % 2], past((b * (GROUPS // 2) + g // 2 + 1) * 16))
                if u == 0:
                    act.wait_ge(acc_done, past(n_in_block))
                act.activation(w_hi[:, g % 2, u], w_raw[:, g % 2, u], ACT.Copy).then_inc(hi_done, 1)

            def sqrt(b):
                act.wait_ge(stats_done, past(b + 1))
                act.activation(std[:], agg[:, :, 1], ACT.Sqrt, bias=eps[:, 0:1]).then_inc(std_done, 1)

            act.wait_ge(eps_set, past(1))
            sqrt(0)
            act.wait_ge(consts_in, past(64))
            act.activation(lr_hi[:], lr_raw, ACT.Copy).then_inc(lr_hi_done, 1)
            for u in range(UNITS):
                act.wait_ge(w_in_slot[0], past(16))
                act.activation(w_hi[:, 0, u], w_raw[:, 0, u], ACT.Copy).then_inc(hi_done, 1)

            def body(b, last):
                for kc in range(KC):
                    act.wait_ge(tr_done, past(b * KC + kc + 1))
                    if kc == 0:
                        act.wait_ge(acc_done, past(b * GROUPS * UNITS))
                    act.activation(xt_hi[:, kc, :], ps_t[:, kc % 2, :], ACT.Copy).then_inc(xt_hi_done, 1)
                for g in range(GROUPS):
                    more = not (last and g == GROUPS - 1)
                    for u in range(UNITS):
                        if u < 2:
                            act.wait_ge(acc_done, past(b * GROUPS * UNITS + g * UNITS + u + 1))
                            act.wait_ge(out_stored[u], past((b * GROUPS + g) * 16))
                            act.activation(out[:, u, :], ps_o[:, u, :], ACT.Copy).then_inc(copied_act, 1)
                        if more:
                            nxt = g + 1
                            split_hi(b * GROUPS * UNITS + g * UNITS, b + nxt // GROUPS, nxt % GROUPS, u)
                    if g == 0:
                        act.wait_ge(lr_done, past(b + 1))
                        act.wait_ge(lr_stored, past(b * 16))
                        act.activation(out_lr[:], ps_lr[:], ACT.Copy).then_inc(lr_copied, 1)
                    if g == 1 and not last:
                        sqrt(b + 1)
            by_blocks(act, NBLK, body)

        @block.vector
        def _(dve):
            def split_lo(b, g, u):
                n = b * GROUPS * UNITS + g * UNITS + u
                dve.wait_ge(hi_done, past(n + 1))
                dve.tensor_tensor(w_lo[:, g % 2, u], w_raw[:, g % 2, u],
                                  w_hi[:, g % 2, u].bitcast(F32), ALU.subtract).then_inc(lo_done, 1)

            def statistics(b):
                dve.wait_ge(x_in, past((b + 1) * 16))
                for t in range(TPB):
                    for h in range(2):
                        ins = dve.bn_stats(stats[:, t, h, :], xb[:, t, h * BLK:(h + 1) * BLK])
                ins.then_inc(ln_step, 1)
                hold(dve, ln_step, past(b * LN_STEPS + 1))
                for t in range(TPB):
                    ins = dve.bn_aggr(agg[:, t, :], stats[:, t].rearrange("p h s -> p (h s)"))
                ins.then_inc(stats_done, 1)

            def normalise(b):
                if isinstance(b, int) and b == 0:
                    dve.wait_ge(consts_in, past(64))
                dve.wait_ge(std_done, past(b + 1))
                dve.reciprocal(rstd[:], std[:]).then_inc(ln_step, 1)
                dve.wait_ge(ln_step, past(b * LN_STEPS + 2))
                for t in range(TPB):
                    dve.tensor_scalar(xb[:, t, :], xb[:, t, :], agg[:, t, 0:1], rstd[:, t:t + 1],
                                      ALU.subtract, ALU.mult).then_inc(ln_step, 1)
                    dve.wait_ge(ln_step, past(b * LN_STEPS + 3 + 3 * t))
                    dve.tensor_tensor(xb[:, t, :], xb[:, t, :], gain[:], ALU.mult).then_inc(ln_step, 1)
                    dve.wait_ge(ln_step, past(b * LN_STEPS + 4 + 3 * t))
                    dve.tensor_tensor(xb[:, t, :], xb[:, t, :], shift[:], ALU.add).then_inc(ln_step, 1)

            dve.memset(eps[:], LN_EPS).then_inc(eps_set, 1)
            statistics(0)
            normalise(0)
            dve.wait_ge(lr_hi_done, past(1))
            dve.tensor_tensor(lr_lo[:], lr_raw, lr_hi[:].bitcast(F32), ALU.subtract).then_inc(lr_lo_done, 1)
            for u in range(UNITS):
                split_lo(0, 0, u)

            def body(b, last):
                for kc in range(KC):
                    dve.wait_ge(xt_hi_done, past(b * KC + kc + 1))
                    dve.tensor_tensor(xt_lo[:, kc, :], ps_t[:, kc % 2, :], xt_hi[:, kc, :].bitcast(F32),
                                      ALU.subtract).then_inc(xt_lo_done, 1)
                for g in range(GROUPS):
                    more = not (last and g == GROUPS - 1)
                    for u in range(UNITS):
                        if u >= 2:
                            dve.wait_ge(acc_done, past(b * GROUPS * UNITS + g * UNITS + u + 1))
                            dve.wait_ge(out_stored[u], past((b * GROUPS + g) * 16))
                            dve.tensor_copy(out[:, u, :], ps_o[:, u, :]).then_inc(copied_dve, 1)
                        if more:
                            nxt = g + 1
                            split_lo(b + nxt // GROUPS, nxt % GROUPS, u)
                    if g == 1 and not last:
                        statistics(b + 1)
                    if g == 2 and not last:
                        normalise(b + 1)
            by_blocks(dve, NBLK, body)

        @block.tensor
        def _(pe):
            def body(b, last):
                pe.wait_ge(ln_step, past((b + 1) * LN_STEPS))
                for kc in range(KC):
                    pe.wait_ge(xt_lo_done, past(b * KC + max(kc - 1, 0) if kc < 2 else b * KC + kc - 1))
                    for t in range(TPB):
                        mm = pe.transpose(ps_t[:, kc % 2, t * P:(t + 1) * P],
                                          xb[:, t, kc * P:(kc + 1) * P], ident[:])
                    mm.then_inc(tr_done, 1)
                pe.wait_ge(xt_lo_done, past((b + 1) * KC))
                pe.wait_ge(lr_lo_done, past(1))
                pe.wait_ge(lr_copied, past(b))
                for kc in range(KC):
                    mm = three_pass(pe, ps_lr[:], (lr_hi[:, kc, :], lr_lo[:, kc, :]),
                                    (xt_hi[:, kc, :], xt_lo[:, kc, :]), kc == 0, kc == KC - 1)
                mm.then_inc(lr_done, 1)
                for g in range(GROUPS):
                    for u in range(UNITS):
                        pe.wait_ge(lo_done, past(b * GROUPS * UNITS + g * UNITS + (u if g < T_GROUPS else UNITS - 1) + 1))
                        pe.wait_ge(copied_act if u < 2 else copied_dve, past(b * GROUPS * 2 + (g - 1) * 2 + u % 2 + 1
                                   if g else b * GROUPS * 2))
                        for kc in range(KC):
                            if g < T_GROUPS:
                                lhs = (w_hi[:, g % 2, u, kc, :], w_lo[:, g % 2, u, kc, :])
                                rhs = (xt_hi[:, kc, :], xt_lo[:, kc, :])
                            else:
                                lhs = (xt_hi[:, kc, u * P:(u + 1) * P], xt_lo[:, kc, u * P:(u + 1) * P])
                                rhs = (w_hi[:, g % 2, :, kc, :], w_lo[:, g % 2, :, kc, :])
                            mm = three_pass(pe, ps_o[:, u, :], lhs, rhs, kc == 0, kc == KC - 1)
                        mm.then_inc(acc_done, 1)
            by_blocks(pe, NBLK, body)


GT = 4
NG = NT // GT
SEQS = ((0, T_PROMPT // CHUNK), (T_PROMPT // CHUNK, NCHUNK))


def gla(nc, qk_t, lr_t, tok_proj, w_gate, b_gate, norm_g, ident_in, reset_in, causal_in, mix_hi, mix_lo):
    with ExitStack() as ctx:
        st = Store(nc, ctx, "gla")
        ident = st.sb("ident", [P, P])
        reset = st.sb("reset", [P, TOK])
        causal = st.sb("causal", [P, 2, P], I32)
        gain = st.sb("gain", [P, DV])
        lr = st.sb("lr", [2 * LOWRANK, TOK])
        wg, bg = st.sb("wg", [2 * LOWRANK, P]), st.sb("bg", [P, 1])
        q, k = st.sb("q", [P, TOK]), st.sb("k", [P, TOK])
        v, gate = st.sb("v", [P, NT, DV]), st.sb("gate", [P, NT, DV])
        z, e = st.sb("z", [P, TOK]), st.sb("e", [P, TOK])
        cum = st.sb("cum", [P, TOK])
        k_in = st.sb("k_in", [P, TOK])
        decay = st.sb("decay", [P, NCHUNK])
        k_tok = st.sb("k_tok", [P, 2, GT, P])
        u = st.sb("u", [P, NCHUNK, DV])
        state = st.sb("state", [P, NCHUNK, DV])
        a_f, a_b = st.sb("a_f", [P, 2, GT, P]), st.sb("a_b", [P, 2, GT, P])
        o = st.sb("o", [P, NT, DV])
        ss, rinv = st.sb("ss", [P, NT]), st.sb("rinv", [P, NT])
        eps = st.sb("eps", [P, 1])
        hi, lo = st.sb("hi", [P, TOK], F32R), st.sb("lo", [P, TOK], F32R)
        ps_w = st.ps("ps_w", [P, 2, BLK])
        ps_k = st.ps("ps_k", [P, BLK])
        ps_u = st.ps("ps_u", [P, 2, BLK])
        ps_f, ps_b = st.ps("ps_f", [P, BLK]), st.ps("ps_b", [P, BLK])
        ps_o = st.ps("ps_o", [P, BLK])

        consts_in, consts_set = st.sem("consts_in"), st.sem("consts_set")
        qk_in, v_in, gate_in, wg_in = (st.sem(n) for n in ("qk_in", "v_in", "gate_in", "wg_in"))
        z_done, z_copied = st.sem("z_done"), st.sem("z_copied")
        soft_done = st.sem("soft_done")
        la_done, cum_done, rest_done = st.sem("la_done"), st.sem("cum_done"), st.sem("rest_done")
        exp_done = st.sem("exp_done")
        qk_done = st.sem("qk_done")
        kt_done, k_tok_done = st.sem("kt_done"), st.sem("k_tok_done")
        u_done, u_copied = st.sem("u_done"), st.sem("u_copied")
        fwd_step, bwd_step = st.sem("fwd_step"), st.sem("bwd_step")
        a_done, a_masked = st.sem("a_done"), st.sem("a_masked")
        o_done, o_copied = st.sem("o_done"), st.sem("o_copied")
        sq_done, ss_done, ms_done, std_done, rinv_done = (
            st.sem(n) for n in ("sq_done", "ss_done", "ms_done", "std_done", "rinv_done"))
        silu_done, norm_step = st.sem("silu_done"), st.sem("norm_step")
        ot_done, hi_done, lo_done = st.sem("ot_done"), st.sem("hi_done"), st.sem("lo_done")
        stored = st.sem("stored")
        STEPS = sum(b - a - 1 for a, b in SEQS)
        NORM = 3
        st.start()
        block = ctx.enter_context(nc.Block())

        @block.sync
        def _(sp):
            sp.dma_start(ident[:], ident_in).then_inc(consts_in, 16)
            sp.dma_start(reset[:], reset_in).then_inc(consts_in, 16)
            sp.dma_start(causal[:], causal_in).then_inc(consts_in, 16)
            sp.dma_start(gain[:], norm_g.partition_broadcast(P)).then_inc(consts_in, 16)
            sp.dma_start(lr[:], lr_t).then_inc(consts_in, 16)
            with sp.Fori(0, GLA_H) as h:
                hold(sp, z_copied, past(h * NBLK))
                sp.dma_start(wg[:], w_gate[h]).then_inc(wg_in, 16)
                sp.dma_start(bg[:], b_gate[h]).then_inc(wg_in, 16)
                hold(sp, qk_done, past(h * 3))
                for half in range(2):
                    rows = slice(half * DK, (half + 1) * DK)
                    sp.dma_start(k[rows, :], qk_t[bass.ds(GLA_H * DK + h * DK, DK), :]).then_inc(qk_in, 16)
                    sp.dma_start(q[rows, :], qk_t[bass.ds(h * DK, DK), :]).then_inc(qk_in, 16)
                hold(sp, o_done, past(h * NG))
                sp.dma_start(v[:], tok_proj[0, :, bass.ds(h * DV, DV)].rearrange("(t p) d -> p t d", p=P)
                             ).then_inc(v_in, 16)
                hold(sp, norm_step, past(h * NORM))
                sp.dma_start(gate[:], tok_proj[1, :, bass.ds(h * DV, DV)].rearrange("(t p) d -> p t d", p=P)
                             ).then_inc(gate_in, 16)
                hold(sp, lo_done, past((h + 1) * NG))
                sp.dma_start(mix_hi[bass.ds(h * DV, DV), :], hi[:].bitcast(F32)).then_inc(stored, 16)
                sp.dma_start(mix_lo[bass.ds(h * DV, DV), :], lo[:].bitcast(F32)).then_inc(stored, 16)
            hold(sp, stored, past(GLA_H * 32))

        @block.gpsimd
        def _(pool):
            pool.memset(a_f[:], 0.0).then_inc(consts_set, 1)
            pool.memset(a_b[:], 0.0).then_inc(consts_set, 1)
            hold(pool, consts_set, past(7 - len(SEQS)))
            for c0, c1 in SEQS:
                pool.memset(state[DK:P, c1 - 1, :], 0.0).then_inc(consts_set, 1)
        @block.scalar
        def _(act):
            act.wait_ge(consts_set, past(7))
            with act.Fori(0, GLA_H) as h:
                act.wait_ge(wg_in, past((h + 1) * 32))
                act.wait_ge(la_done, past(h))
                for b in range(NBLK):
                    act.wait_ge(z_done, past(h * NBLK + b + 1))
                    act.activation(z[:, b * BLK:(b + 1) * BLK], ps_w[:, b % 2, :], ACT.Identity,
                                   bias=bg[:, 0:1]).then_inc(z_copied, 1)
                act.wait_ge(z_copied, past((h + 1) * NBLK))
                act.wait_ge(kt_done, past(h * NG))
                act.wait_ge(ss_done, past(h))
                act.activation(e[:], z[:], ACT.Abs).then_inc(soft_done, 1)
                act.wait_ge(soft_done, past(h * 3 + 1))
                act.activation(e[:], e[:], ACT.Exp, scale=-1.0).then_inc(soft_done, 1)
                act.wait_ge(soft_done, past(h * 3 + 2))
                act.activation(e[:], e[:], ACT.Ln, bias=1.0).then_inc(soft_done, 1)
                act.wait_ge(rest_done, past((h + 1) * 2))
                act.activation(decay[0:DK, :], cum[0:DK, CHUNK - 1::CHUNK], ACT.Exp, scale=1.0 / TAU)
                act.activation(decay[DK:P, :], cum[DK:P, 0::CHUNK], ACT.Exp, scale=1.0 / TAU).then_inc(exp_done, 1)
                act.activation(e[:], e[:], ACT.Exp, scale=1.0 / TAU).then_inc(exp_done, 1)
                act.activation(k_in[:], cum[:], ACT.Exp, scale=-1.0 / TAU).then_inc(exp_done, 1)
                act.wait_ge(exp_done, past(h * 4 + 3))
                act.activation(cum[:], cum[:], ACT.Exp, scale=1.0 / TAU).then_inc(exp_done, 1)
                for g in range(NG):
                    act.wait_ge(kt_done, past(h * NG + g + 1))
                    if g >= 2:
                        act.wait_ge(u_done, past(h * 2 * NG + 2 * (g - 1)))
                    act.activation(k_tok[:, g % 2], ps_k[:], ACT.Copy).then_inc(k_tok_done, 1)
                for g in range(NG):
                    act.wait_ge(o_done, past(h * NG + g + 1))
                    act.activation(o[:, g * GT:(g + 1) * GT, :], ps_o[:], ACT.Copy).then_inc(o_copied, 1)
                act.wait_ge(o_copied, past((h + 1) * NG))
                act.activation(e[:], o[:].rearrange("p t d -> p (t d)"), ACT.Square).then_inc(sq_done, 1)
                act.wait_ge(gate_in, past((h + 1) * 16))
                act.activation(gate[:], gate[:], ACT.Silu).then_inc(silu_done, 1)
                act.wait_ge(ss_done, past(h + 1))
                act.activation(rinv[:], ss[:], ACT.Sqrt, scale=1.0 / DV, bias=eps[:, 0:1]).then_inc(std_done, 1)
                act.wait_ge(stored, past(h * 32))
                for g in range(NG):
                    act.wait_ge(ot_done, past(h * NG + g + 1))
                    act.activation(hi[:, g * BLK:(g + 1) * BLK], ps_w[:, g % 2, :], ACT.Copy).then_inc(hi_done, 1)

        @block.vector
        def _(dve):
            dve.memset(eps[:], RMS_EPS).then_inc(consts_set, 1)
            for c0, c1 in SEQS:
                dve.memset(state[0:DK, c0, :], 0.0).then_inc(consts_set, 1)
            dve.wait_ge(consts_set, past(7))
            dve.wait_ge(consts_in, past(16 * 5))
            with dve.Fori(0, GLA_H) as h:
                dve.wait_ge(soft_done, past((h + 1) * 3))
                dve.scalar_tensor_tensor(z[:], z[:], 0.0, e[:], ALU.min, ALU.subtract).then_inc(la_done, 1)
                dve.wait_ge(la_done, past(h + 1))
                dve.wait_ge(o_done, past(h * NG))
                dve.tensor_tensor_scan(cum[0:DK, :], reset[0:DK, :], z[0:DK, :], 0.0,
                                       ALU.mult, ALU.add).then_inc(cum_done, 1)
                dve.tensor_tensor_scan(cum[DK:P, ::-1], reset[DK:P, :], z[DK:P, ::-1], 0.0,
                                       ALU.mult, ALU.add).then_inc(cum_done, 1)
                dve.wait_ge(cum_done, past((h + 1) * 2))
                for rows, last in ((slice(0, DK), CHUNK - 1), (slice(DK, P), 0)):
                    by_chunk = cum[rows, :].rearrange("p (c i) -> p c i", i=CHUNK)
                    whole = by_chunk[:, :, last:last + 1].to_broadcast([DK, NCHUNK, CHUNK])
                    dve.tensor_tensor(e[rows, :].rearrange("p (c i) -> p c i", i=CHUNK), whole, by_chunk,
                                      ALU.subtract).then_inc(rest_done, 1)
                dve.wait_ge(qk_in, past((h + 1) * 64))
                dve.wait_ge(exp_done, past(h * 4 + 2))
                dve.tensor_tensor(e[:], k[:], e[:], ALU.mult).then_inc(qk_done, 1)
                dve.wait_ge(exp_done, past(h * 4 + 3))
                dve.tensor_tensor(k_in[:], k[:], k_in[:], ALU.mult).then_inc(qk_done, 1)
                dve.wait_ge(exp_done, past(h * 4 + 4))
                dve.scalar_tensor_tensor(cum[:], q[:], DK ** -0.5, cum[:], ALU.mult, ALU.mult).then_inc(qk_done, 1)

                def mask(g):
                    if g >= 2:
                        dve.wait_ge(o_done, past(h * NG + g - 1))
                    hold(dve, a_done, past(h * NG + g + 1))
                    for d, (ps, a) in enumerate(((ps_f, a_f), (ps_b, a_b))):
                        m = causal[:, d:d + 1, :].to_broadcast([P, GT, P])
                        ins = dve.copy_predicated(a[:, g % 2], m, ps[:].rearrange("p (t i) -> p t i", i=P))
                    ins.then_inc(a_masked, 1)

                for g in range(NG):
                    for half in range(2):
                        dve.wait_ge(u_done, past(h * 2 * NG + 2 * g + half + 1))
                        c = 2 * g * GT
                        dve.tensor_copy(u[:, c + half:c + 2 * GT:2, :],
                                        ps_u[:, half, :].rearrange("p (t d) -> p t d", d=DV)).then_inc(u_copied, 1)
                mask(0)
                dve.wait_ge(u_copied, past((h + 1) * 2 * NG))
                n = 0
                for c0, c1 in SEQS:
                    for j in range(c1 - c0 - 1):
                        if n:
                            dve.wait_ge(fwd_step, past(h * STEPS + n))
                        c = c0 + j
                        dve.scalar_tensor_tensor(state[0:DK, c + 1, :], state[0:DK, c, :],
                                                 decay[0:DK, c:c + 1], u[0:DK, c, :],
                                                 ALU.mult, ALU.add).then_inc(fwd_step, 1)
                        if n:
                            dve.wait_ge(bwd_step, past(h * STEPS + n))
                        c = c1 - 1 - j
                        dve.scalar_tensor_tensor(state[DK:P, c - 1, :], state[DK:P, c, :],
                                                 decay[DK:P, c:c + 1], u[DK:P, c, :],
                                                 ALU.mult, ALU.add).then_inc(bwd_step, 1)
                        n += 1
                for g in range(1, NG):
                    mask(g)
                dve.wait_ge(sq_done, past(h + 1))
                dve.tensor_reduce(ss[:], e[:].rearrange("p (t d) -> p t d", d=DV), AX_X, ALU.add).then_inc(ss_done, 1)
                dve.wait_ge(std_done, past(h + 1))
                dve.reciprocal(rinv[:], rinv[:]).then_inc(rinv_done, 1)
                dve.wait_ge(rinv_done, past(h + 1))
                wide = rinv[:].rearrange("p (t a) -> p t a", a=1).to_broadcast([P, NT, DV])
                dve.tensor_tensor(o[:], o[:], wide, ALU.mult).then_inc(norm_step, 1)
                dve.wait_ge(norm_step, past(h * NORM + 1))
                wide = gain[:].rearrange("p (a d) -> p a d", a=1).to_broadcast([P, NT, DV])
                dve.tensor_tensor(o[:], o[:], wide, ALU.mult).then_inc(norm_step, 1)
                dve.wait_ge(norm_step, past(h * NORM + 2))
                dve.wait_ge(silu_done, past(h + 1))
                dve.tensor_tensor(o[:], o[:], gate[:], ALU.mult).then_inc(norm_step, 1)
                for g in range(NG):
                    dve.wait_ge(hi_done, past(h * NG + g + 1))
                    dve.tensor_tensor(lo[:, g * BLK:(g + 1) * BLK], ps_w[:, g % 2, :],
                                      hi[:, g * BLK:(g + 1) * BLK].bitcast(F32), ALU.subtract).then_inc(lo_done, 1)

        @block.tensor
        def _(pe):
            pe.wait_ge(consts_in, past(16 * 5))
            with pe.Fori(0, GLA_H) as h:
                pe.wait_ge(wg_in, past((h + 1) * 32))
                pe.wait_ge(lo_done, past(h * NG))
                for b in range(NBLK):
                    if b >= 2:
                        pe.wait_ge(z_copied, past(h * NBLK + b - 1))
                    pe.matmul(ps_w[:, b % 2, :], wg[:], lr[:, b * BLK:(b + 1) * BLK],
                              start=True, stop=True).then_inc(z_done, 1)
                pe.wait_ge(qk_done, past(h * 3 + 1))
                pe.wait_ge(v_in, past((h + 1) * 16))

                def keys_by_token(g):
                    pe.wait_ge(k_tok_done, past(h * NG + g))
                    for i in range(GT):
                        t = g * GT + i
                        mm = pe.transpose(ps_k[:, i * P:(i + 1) * P], e[:, t * P:(t + 1) * P], ident[:])
                    mm.then_inc(kt_done, 1)

                def chunk_sums(g):
                    pe.wait_ge(k_tok_done, past(h * NG + g + 1))
                    pe.wait_ge(u_copied, past(h * 2 * NG + 2 * g))
                    for i in range(GT):
                        for c in range(2):
                            rows = slice(c * CHUNK, (c + 1) * CHUNK)
                            mm = pe.matmul(ps_u[:, c, i * DV:(i + 1) * DV], k_tok[rows, g % 2, i, :],
                                           v[rows, g * GT + i, :], start=True, stop=True)
                            if i == GT - 1:
                                mm.then_inc(u_done, 1)

                def scores(g):
                    pe.wait_ge(a_masked, past(h * NG + g))
                    for rows, ps in ((slice(0, DK), ps_f), (slice(DK, P), ps_b)):
                        for i in range(GT):
                            cols = slice((g * GT + i) * P, (g * GT + i + 1) * P)
                            mm = pe.matmul(ps[:, i * P:(i + 1) * P], k_in[rows, cols], cum[rows, cols],
                                           start=True, stop=True)
                    mm.then_inc(a_done, 1)

                def outputs(g):
                    pe.wait_ge(a_masked, past(h * NG + g + 1))
                    pe.wait_ge(o_copied, past(h * NG + g))
                    for i in range(GT):
                        t = g * GT + i
                        out = ps_o[:, i * P:(i + 1) * P]
                        pe.matmul(out, a_f[:, g % 2, i, :], v[:, t, :], start=True, stop=False)
                        pe.matmul(out, a_b[:, g % 2, i, :], v[:, t, :], start=False, stop=True)
                        for c in range(2):
                            rows = slice(c * CHUNK, (c + 1) * CHUNK)
                            col = t * P + c * CHUNK
                            mm = pe.matmul(ps_o[rows, i * P:(i + 1) * P], cum[:, col:col + CHUNK],
                                           state[:, 2 * t + c, :], start=False, stop=True, skip_group_check=True)
                    mm.then_inc(o_done, 1)

                keys_by_token(0)
                for g in range(NG):
                    chunk_sums(g)
                    if g + 1 < NG:
                        keys_by_token(g + 1)
                pe.wait_ge(qk_done, past(h * 3 + 3))
                scores(0)
                pe.wait_ge(fwd_step, past((h + 1) * STEPS))
                pe.wait_ge(bwd_step, past((h + 1) * STEPS))
                for g in range(NG):
                    if g + 1 < NG:
                        scores(g + 1)
                    outputs(g)
                pe.wait_ge(norm_step, past((h + 1) * NORM))
                for g in range(NG):
                    pe.wait_ge(lo_done, past(h * NG + g - 1 if g >= 2 else h * NG))
                    for i in range(GT):
                        mm = pe.transpose(ps_w[:, g % 2, i * P:(i + 1) * P], o[:, g * GT + i, :], ident[:])
                    mm.then_inc(ot_done, 1)


NQB = GRID_W // QB_C
ROWS_U = BLK // GRID_W
KG = P // BAND
NKG = TOK // GRID_W // KG
BAND_AT = (0, 8, 24, 32)
BIAS_ROWS, BIAS_COLS = 16, 48
PAD_R, PAD_C = 4, 16
RPB_R, RPB_C = ROWS_U - 1 + BIAS_ROWS, QB_C - 1 + BIAS_COLS
COL_AT = (16, 8, 8, 0)
COL_TYPE = (0, 1, 1, 2)
UNITS_NA = ((0, 2, 4, 0), (2, 3, 4, 8), (3, 4, 0, 20), (5, 4, 0, 20), (7, 3, 0, 36))
TABLE_ROWS = 48
NU = len(UNITS_NA)


def natten_masks():
    a, c = np.divmod(np.arange(P), QB_C)
    col = np.full((P, 3, BAND), MASKED, np.float32)
    kc = np.arange(BAND)[None, :]
    for t, start in enumerate((np.maximum(c - 8, 0), c, np.minimum(c + 8, 16))):
        col[:, t][(kc >= start[:, None]) & (kc < start[:, None] + WIN_C)] = 0.0
    row = np.full((P, TABLE_ROWS), MASKED, np.float32)
    for at, e0, n, start in ((0, 4, 8, np.full(P, 4)), (8, 4, 12, np.maximum(a, 4)),
                             (20, 0, 16, a), (36, 0, 12, np.minimum(a, 4))):
        e = e0 + np.arange(n)[None, :]
        row[:, at:at + n][(e >= start[:, None]) & (e < start[:, None] + WIN_R)] = 0.0
    return col, row


def natten(nc, qk_t, tok_proj, rpb_pad, col_mask, row_mask, ident_in, rpb_rep, mix_hi, mix_lo):
    with ExitStack() as ctx:
        st = Store(nc, ctx, "natten")
        ident = st.sb("ident", [P, P])
        cmask, rmask = st.sb("cmask", [P, 3, BAND]), st.sb("rmask", [P, TABLE_ROWS])
        mask = st.sb("mask", [P, 3, TABLE_ROWS, BAND])
        bias = st.sb("bias", [P, BIAS_ROWS, BIAS_COLS])
        table = st.sb("table", [P, 2, 3, TABLE_ROWS, BAND])
        q_raw, k = st.sb("q_raw", [P, TOK]), st.sb("k", [P, TOK])
        q = st.sb("q", [P, NU, NQB, P])
        v = st.sb("v", [P, 2, NKG, NQB, DH])
        s = st.sb("s", [P, NU, NQB, BLK])
        pt = st.sb("pt", [P, NQB, BLK])
        mx, nmx = st.sb("mx", [P, 2 * NU, NQB]), st.sb("nmx", [P, 2 * NU, NQB])
        den, rden = st.sb("den", [P, 2 * NU, NQB]), st.sb("rden", [P, 2 * NU, NQB])
        hi, lo = st.sb("hi", [P, TOK], F32R), st.sb("lo", [P, TOK], F32R)
        ps_s = st.ps("ps_s", [P, NQB, BLK])
        ps_t = st.ps("ps_t", [P, 2, BLK])
        ps_o = st.ps("ps_o", [P, 2, BLK])

        consts_in, mask_set = st.sem("consts_in"), st.sem("mask_set")
        rep_done = st.sem("rep_done")
        bias_in, table_done = st.sem("bias_in"), st.sem("table_done")
        q_in, k_in, v_in, stored = ([st.sem(f"{n}_{side}") for side in range(2)]
                                    for n in ("q_in", "k_in", "v_in", "stored"))
        q_set = st.sem("q_set")
        s_done, biased, nmx_done = st.sem("s_done"), st.sem("biased"), st.sem("nmx_done")
        exp_done, rden_done, p_done = st.sem("exp_done"), st.sem("rden_done"), st.sem("p_done")
        t_done = st.sem("t_done")
        pt_act, pt_dve = st.sem("pt_act"), st.sem("pt_dve")
        o_done, hi_done, lo_done = (st.sem(n) for n in ("o_done", "hi_done", "lo_done"))
        SC = NU * NQB
        TABLES = 12
        PAIRS = NA_H // 2
        NU2 = 2 * NU
        st.start()
        block = ctx.enter_context(nc.Block())

        def half_of(side):
            return slice(side * DH, (side + 1) * DH)

        @block.sync
        def _(sp):
            def load_bias(h):
                for a in range(ROWS_U):
                    base = rpb_rep[bass.ds(h, 1), a]
                    src = bass.AP(tensor=base.tensor, offset=base.offset + QB_C - 1,
                                  ap=[[BIAS_ROWS * RPB_C - 1, QB_C], [RPB_C, BIAS_ROWS], [1, BIAS_COLS]])
                    sp.dma_start(bias[a * QB_C:(a + 1) * QB_C], src).then_inc(bias_in, 16)

            def load_q(h, side):
                sp.dma_start(q_raw[half_of(side), :], qk_t[bass.ds(4 * P + h * DH, DH), :]).then_inc(q_in[side], 16)

            def load_k(h, side):
                sp.dma_start(k[half_of(side), :], qk_t[bass.ds(8 * P + h * DH, DH), :]).then_inc(k_in[side], 16)

            def load_v(h, side):
                by_row = tok_proj[2, :, bass.ds(h * DH, DH)].rearrange("(g a c) d -> a c g d", a=KG, c=GRID_W)
                for cb in range(NQB):
                    for a in range(KG):
                        sp.dma_start(v[a * BAND:(a + 1) * BAND, side, :, cb, :],
                                     by_row[a, BAND_AT[cb]:BAND_AT[cb] + BAND]).then_inc(v_in[side], 16)

            sp.dma_start(rmask[:], row_mask).then_inc(consts_in, 16)
            sp.dma_start(cmask[:], col_mask).then_inc(consts_in, 16)
            for a in range(ROWS_U):
                src = rpb_pad[:, ROWS_U - 1 - a:ROWS_U - 1 - a + BIAS_ROWS, :].rearrange("h (o r) x -> h o (r x)", o=1)
                sp.dma_start(rpb_rep[:, a], src.to_broadcast([NA_H, QB_C, BIAS_ROWS * RPB_C])).then_inc(rep_done, 16)
            load_q(0, 0)
            load_k(0, 0)
            sp.dma_start(ident[:], ident_in).then_inc(consts_in, 16)
            hold(sp, rep_done, past(16 * ROWS_U))
            load_bias(0)
            load_v(0, 0)

            def body(pair, last):
                for side in range(2):
                    h = pair * 2 + side
                    if not (last and side):
                        hold(sp, table_done, past((h + 1) * TABLES))
                        load_bias(h + 1)
                        hold(sp, q_set, past(h))
                        load_q(h + 1, 1 - side)
                        hold(sp, s_done, past(h * SC))
                        load_k(h + 1, 1 - side)
                        hold(sp, o_done, past(h * NU))
                        load_v(h + 1, 1 - side)
                    hold(sp, lo_done, past((h + 1) * NU))
                    rows = bass.ds(4 * P + h * DH, DH)
                    sp.dma_start(mix_hi[rows, :], hi[half_of(side), :].bitcast(F32)).then_inc(stored[side], 16)
                    sp.dma_start(mix_lo[rows, :], lo[half_of(side), :].bitcast(F32)).then_inc(stored[side], 16)
            by_blocks(sp, PAIRS, body)
            for side in range(2):
                hold(sp, stored[side], past(PAIRS * 32))

        @block.gpsimd
        def _(pool):
            hold(pool, consts_in, past(48))
            for t in range(3):
                pool.tensor_tensor(mask[:, t], rmask[:].rearrange("p (r a) -> p r a", a=1).to_broadcast([P, TABLE_ROWS, BAND]),
                                   cmask[:, t:t + 1, :].to_broadcast([P, TABLE_ROWS, BAND]), ALU.add).then_inc(mask_set, 1)
            hold(pool, mask_set, past(3))

            def tables(h, side):
                hold(pool, bias_in, past((h + 1) * 16 * ROWS_U))
                for t, x in enumerate((16, 8, 0)):
                    for at, e0, n in ((0, 4, 8), (8, 4, 12), (20, 0, 16), (36, 0, 12)):
                        pool.tensor_tensor(table[:, side, t, at:at + n, :], bias[:, e0:e0 + n, x:x + BAND],
                                           mask[:, t, at:at + n, :], ALU.add).then_inc(table_done, 1)

            tables(0, 0)
            tables(1, 1)
            with pool.Fori(0, PAIRS - 1) as pair:
                for side in range(2):
                    h = pair * 2 + side
                    hold(pool, biased, past((h + 1) * SC))
                    tables(h + 2, side)

        @block.scalar
        def _(act):
            def set_queries(h, pair, side):
                rows = half_of(side)
                act.wait_ge(q_in[side], past((pair + 1) * 16))
                for u in range(NU):
                    ins = act.activation(q[rows, u].rearrange("p b (a c) -> p a b c", c=QB_C),
                                         q_raw[rows, u * BLK:(u + 1) * BLK].rearrange("p (a b c) -> p a b c", b=NQB, c=QB_C),
                                         ACT.Copy, scale=DH ** -0.5)
                ins.then_inc(q_set, 1)

            def exps(unit, j, blocks):
                n = UNITS_NA[j % NU][1] * P
                act.wait_ge(nmx_done, past(unit + 1))
                for cb in blocks:
                    act.activation(s[:, j % NU, cb, :n], s[:, j % NU, cb, :n], ACT.Exp, bias=nmx[:, j, cb:cb + 1],
                                   accum_out=den[:, j, cb:cb + 1]).then_inc(exp_done, 1)

            set_queries(0, 0, 0)
            exps(0, 0, range(NQB))

            def body(pair, last):
                for j in range(NU2):
                    unit, side, u = pair * NU2 + j, j // NU, j % NU
                    n = UNITS_NA[u][1] * P
                    for cb in range(0, NQB, 2):
                        act.wait_ge(t_done, past(unit * NQB + cb + 1))
                        act.wait_ge(o_done, past(unit))
                        act.activation(pt[:, cb, :n], ps_t[:, cb % 2, :n], ACT.Copy).then_inc(pt_act, 1)
                        if not (last and j == NU2 - 1):
                            exps(unit + 1, (j + 1) % NU2, (cb, cb + 1))
                    if u == 1 and not (last and side):
                        h = pair * 2 + side
                        act.wait_ge(s_done, past(h * SC))
                        set_queries(h + 1, pair + side, 1 - side)
                    act.wait_ge(o_done, past(unit + 1))
                    if u == 0:
                        act.wait_ge(stored[side], past(pair * 32))
                    rows = half_of(side)
                    act.activation(hi[rows, u * BLK:(u + 1) * BLK].rearrange("p (a b c) -> p b a c", b=NQB, c=QB_C),
                                   ps_o[rows, j % 2, :].rearrange("p (b a c) -> p b a c", b=NQB, c=QB_C),
                                   ACT.Copy).then_inc(hi_done, 1)
            by_blocks(act, PAIRS, body)

        @block.vector
        def _(dve):
            def add_bias(unit, j, cb):
                _, groups, _, at = UNITS_NA[j % NU]
                n, side = groups * P, j // NU
                hold(dve, s_done, past(unit * NQB + cb + 1))
                bias_u = table[:, side, COL_TYPE[cb], at:at + groups * KG, :].rearrange("p r c -> p (r c)")
                dve.tensor_tensor_reduce(s[:, j % NU, cb, :n], ps_s[:, cb, :n], bias_u, 1.0, -3.0e38,
                                         ALU.add, ALU.max, mx[:, j, cb:cb + 1]).then_inc(biased, 1)

            def negate_max(unit, j):
                dve.wait_ge(biased, past((unit + 1) * NQB))
                dve.tensor_scalar(nmx[:, j, :], mx[:, j, :], -1.0, None, ALU.mult).then_inc(nmx_done, 1)

            def normalise(unit, j, cb):
                n = UNITS_NA[j % NU][1] * P
                dve.wait_ge(exp_done, past(unit * NQB + cb + 2))
                dve.reciprocal(rden[:, j, cb:cb + 2], den[:, j, cb:cb + 2]).then_inc(rden_done, 1)
                dve.wait_ge(rden_done, past(unit * 2 + cb // 2 + 1))
                for i in (cb, cb + 1):
                    dve.tensor_scalar(s[:, j % NU, i, :n], s[:, j % NU, i, :n], rden[:, j, i:i + 1], None,
                                      ALU.mult).then_inc(p_done, 1)

            dve.wait_ge(table_done, past(TABLES))
            for unit in range(2):
                for cb in range(NQB):
                    add_bias(unit, unit, cb)
                negate_max(unit, unit)
            for cb in (0, 2):
                normalise(0, 0, cb)

            def body(pair, last):
                for j in range(NU2):
                    unit, side, u = pair * NU2 + j, j // NU, j % NU
                    more, more2 = (not (last and j + ahead >= NU2) for ahead in (1, 2))
                    n = UNITS_NA[u][1] * P
                    if u == NU - 2 and more2:
                        dve.wait_ge(table_done, past((pair * 2 + side + 2) * TABLES))
                    for cb in (1, 3):
                        if cb == 3 and more2:
                            add_bias(unit + 2, (j + 2) % NU2, 1)
                        dve.wait_ge(t_done, past(unit * NQB + cb + 1))
                        dve.wait_ge(o_done, past(unit))
                        dve.tensor_copy(pt[:, cb, :n], ps_t[:, cb % 2, :n]).then_inc(pt_dve, 1)
                        if more2:
                            add_bias(unit + 2, (j + 2) % NU2, cb - 1)
                        if more:
                            normalise(unit + 1, (j + 1) % NU2, cb - 1)
                    if more2:
                        add_bias(unit + 2, (j + 2) % NU2, 3)
                        negate_max(unit + 2, (j + 2) % NU2)
                    dve.wait_ge(hi_done, past(unit + 1))
                    view, rows = "p (a b c) -> p b a c", half_of(side)
                    dve.tensor_tensor(lo[rows, u * BLK:(u + 1) * BLK].rearrange(view, b=NQB, c=QB_C),
                                      ps_o[rows, j % 2, :].rearrange("p (b a c) -> p b a c", b=NQB, c=QB_C),
                                      hi[rows, u * BLK:(u + 1) * BLK].bitcast(F32).rearrange(view, b=NQB, c=QB_C),
                                      ALU.subtract).then_inc(lo_done, 1)
            by_blocks(dve, PAIRS, body)

        @block.tensor
        def _(pe):
            def inputs(pair, side):
                pe.wait_ge(q_set, past(pair * 2 + side + 1))
                pe.wait_ge(k_in[side], past((pair + 1) * 16))

            def scores(unit, j, cb, first_ever=False):
                first, groups, _, _ = UNITS_NA[j % NU]
                side = j // NU
                keys = k[half_of(side), first * KG * GRID_W:(first + groups) * KG * GRID_W]
                keys = keys.rearrange("p (r c) -> p r c", c=GRID_W)
                if not first_ever:
                    pe.wait_ge(biased, past((unit - 1) * NQB + cb + 1))
                pe.matmul(ps_s[:, cb, :groups * P], q[half_of(side), j % NU, cb, :],
                          keys[:, :, BAND_AT[cb]:BAND_AT[cb] + BAND], start=True, stop=True).then_inc(s_done, 1)

            def turn(unit, j, cb):
                groups = UNITS_NA[j % NU][1]
                pe.wait_ge(p_done, past(unit * NQB + cb + 1))
                pe.wait_ge(pt_dve if cb % 2 else pt_act, past(unit * 2 + cb // 2))
                for g in range(groups):
                    mm = pe.transpose(ps_t[:, cb % 2, g * P:(g + 1) * P],
                                      s[:, j % NU, cb, g * P:(g + 1) * P], ident[:])
                mm.then_inc(t_done, 1)

            def weigh_values(unit, j, cb):
                first, groups, _, _ = UNITS_NA[j % NU]
                rows, side = half_of(j // NU), j // NU
                pe.wait_ge(pt_dve if cb % 2 else pt_act, past(unit * 2 + cb // 2 + 1))
                for g in range(groups):
                    mm = pe.matmul(ps_o[rows, j % 2, cb * P:(cb + 1) * P], v[:, side, first + g, cb, :],
                                   pt[:, cb, g * P:(g + 1) * P], start=(g == 0), stop=(g == groups - 1))
                return mm

            inputs(0, 0)
            for unit in range(2):
                for cb in range(NQB):
                    scores(unit, unit, cb, first_ever=unit == 0)
            pe.wait_ge(consts_in, past(48))

            def body(pair, last):
                for j in range(NU2):
                    unit, side, u = pair * NU2 + j, j // NU, j % NU
                    ahead = not (last and j + 2 >= NU2)
                    if u == NU - 2 and ahead:
                        inputs(pair + side, 1 - side)
                    if u == 0:
                        pe.wait_ge(v_in[side], past((pair + 1) * 16 * NQB * KG))
                    turn(unit, j, 0)
                    pe.wait_ge(lo_done, past(unit - 1 if j else unit))
                    for cb in range(NQB):
                        if cb + 1 < NQB:
                            turn(unit, j, cb + 1)
                        if ahead:
                            scores(unit + 2, (j + 2) % NU2, cb)
                        mm = weigh_values(unit, j, cb)
                    mm.then_inc(o_done, 1)
            by_blocks(pe, PAIRS, body)


HALF = D // 2


def mix_out(nc, xln, mix_hi, mix_lo, w_out, ln_g, ln_b, ident_in, x1, x1t_hi, x1t_lo):
    with ExitStack() as ctx:
        st = Store(nc, ctx, "mix_out")
        ident = st.sb("ident", [P, P])
        gain, shift = st.sb("gain", [P, D]), st.sb("shift", [P, D])
        w_raw = st.sb("w_raw", [P, KC, D])
        w_hi, w_lo = st.sb("w_hi", [P, KC, D], F32R), st.sb("w_lo", [P, KC, D], F32R)
        m_hi, m_lo = st.sb("m_hi", [P, TPB, KC, P], F32R), st.sb("m_lo", [P, TPB, KC, P], F32R)
        y = st.sb("y", [P, TPB, D])
        stats, agg = st.sb("stats", [P, 2, 6]), st.sb("agg", [P, 2])
        std, rstd, eps = st.sb("std", [P, 1]), st.sb("rstd", [P, 1]), st.sb("eps", [P, 1])
        t_hi, t_lo = st.sb("t_hi", [P, KC, P], F32R), st.sb("t_lo", [P, KC, P], F32R)
        ps_m = st.ps("ps_m", [P, 2, 2, HALF])
        ps_t = st.ps("ps_t", [P, 2, BLK])

        consts_in, eps_set = st.sem("consts_in"), st.sem("eps_set")
        w_in = [st.sem(f"w_in_{kc}") for kc in range(0, KC, 2)]
        hi_done, lo_done = st.sem("hi_done"), st.sem("lo_done")
        m_in = [st.sem(f"m_in_{t}") for t in range(TPB)]
        y_in = [st.sem(f"y_in_{t}") for t in range(TPB)]
        mix_done, added = st.sem("mix_done"), st.sem("added")
        var_done, std_done, ln_step = st.sem("var_done"), st.sem("std_done"), st.sem("ln_step")
        tr_done, t_hi_done, t_lo_done = st.sem("tr_done"), st.sem("t_hi_done"), st.sem("t_lo_done")
        y_stored = [st.sem(f"y_stored_{t}") for t in range(TPB)]
        t_stored = st.sem("t_stored")
        STEP = 5
        st.start()
        block = ctx.enter_context(nc.Block())

        @block.sync
        def _(sp):

            def load(b, t):
                cols = bass.ds(b * BLK + t * P, P)
                for src, dst in ((mix_hi, m_hi), (mix_lo, m_lo)):
                    sp.dma_start(dst[:, t].bitcast(F32), src[:, cols].rearrange("(c p) n -> p c n", p=P)
                                 ).then_inc(m_in[t], 16)
                sp.dma_start(y[:, t, :], xln[cols, :]).then_inc(y_in[t], 16)

            def body(b, last):
                for t in range(TPB):
                    cols = bass.ds(b * BLK + t * P, P)
                    hold(sp, ln_step, past((b * TPB + t + 1) * STEP))
                    sp.dma_start(x1[cols, :], y[:, t, :]).then_inc(y_stored[t], 16)
                    hold(sp, t_lo_done, past((b * TPB + t + 1) * 2))
                    for src, dst in ((t_hi, x1t_hi), (t_lo, x1t_lo)):
                        sp.dma_start(dst[:, cols].rearrange("(c p) n -> p c n", p=P), src[:].bitcast(F32)
                                     ).then_inc(t_stored, 16)
                    if not last:
                        hold(sp, y_stored[t], past((b + 1) * 16))
                        load(b + 1, t)

            for kc in range(0, KC, 2):
                sp.dma_start(w_raw[:, kc:kc + 2], w_out[:, kc:kc + 2]).then_inc(w_in[kc // 2], 16)
                if kc == 0:
                    load(0, 0)
            sp.dma_start(gain[:], ln_g.partition_broadcast(P)).then_inc(consts_in, 16)
            sp.dma_start(shift[:], ln_b.partition_broadcast(P)).then_inc(consts_in, 16)
            sp.dma_start(ident[:], ident_in).then_inc(consts_in, 16)
            for t in range(1, TPB):
                load(0, t)
            by_blocks(sp, NBLK, body)
            for sem in y_stored:
                hold(sp, sem, past(NBLK * 16))
            hold(sp, t_stored, past(NT * 32))

        @block.scalar
        def _(act):
            for kc in range(KC):
                act.wait_ge(w_in[kc // 2], past(16))
                act.activation(w_hi[:, kc], w_raw[:, kc], ACT.Copy).then_inc(hi_done, 1)
            act.wait_ge(eps_set, past(1))

            with act.Fori(0, NBLK) as b:
                for t in range(TPB):
                    n = b * TPB + t
                    act.wait_ge(var_done, past(n + 1))
                    act.activation(std[:], agg[:, 1:2], ACT.Sqrt, bias=eps[:, 0:1]).then_inc(std_done, 1)
                    for half in range(2):
                        act.wait_ge(tr_done, past(n * 2 + half + 1))
                        if half == 0:
                            act.wait_ge(t_stored, past(n * 32))
                        act.activation(t_hi[:, half * 4:half * 4 + 4, :], ps_t[:, half, :], ACT.Copy).then_inc(t_hi_done, 1)

        @block.vector
        def _(dve):
            dve.memset(eps[:], LN_EPS).then_inc(eps_set, 1)
            for kc in range(KC):
                dve.wait_ge(hi_done, past(kc + 1))
                dve.tensor_tensor(w_lo[:, kc], w_raw[:, kc], w_hi[:, kc].bitcast(F32), ALU.subtract).then_inc(lo_done, 1)
            dve.wait_ge(consts_in, past(48))
            with dve.Fori(0, NBLK) as b:
                for t in range(TPB):
                    n = b * TPB + t
                    dve.wait_ge(y_in[t], past((b + 1) * 16))
                    dve.wait_ge(mix_done, past(n + 1))
                    for half in range(2):
                        cols = slice(half * HALF, (half + 1) * HALF)
                        dve.scalar_tensor_tensor(y[:, t, cols], y[:, t, cols], ALPHA, ps_m[:, t % 2, half, :],
                                                 ALU.mult, ALU.add).then_inc(added, 1)
                    dve.wait_ge(added, past((n + 1) * 2))
                    for half in range(2):
                        ins = dve.bn_stats(stats[:, half, :], y[:, t, half * HALF:(half + 1) * HALF])
                    ins.then_inc(ln_step, 1)
                    hold(dve, ln_step, past(n * STEP + 1))
                    dve.bn_aggr(agg[:], stats[:].rearrange("p h s -> p (h s)")).then_inc(var_done, 1)
                    dve.wait_ge(std_done, past(n + 1))
                    dve.reciprocal(rstd[:], std[:]).then_inc(ln_step, 1)
                    dve.wait_ge(ln_step, past(n * STEP + 2))
                    dve.tensor_scalar(y[:, t, :], y[:, t, :], agg[:, 0:1], rstd[:, 0:1],
                                      ALU.subtract, ALU.mult).then_inc(ln_step, 1)
                    dve.wait_ge(ln_step, past(n * STEP + 3))
                    dve.tensor_tensor(y[:, t, :], y[:, t, :], gain[:], ALU.mult).then_inc(ln_step, 1)
                    dve.wait_ge(ln_step, past(n * STEP + 4))
                    dve.tensor_tensor(y[:, t, :], y[:, t, :], shift[:], ALU.add).then_inc(ln_step, 1)
                    for half in range(2):
                        dve.wait_ge(t_hi_done, past(n * 2 + half + 1))
                        dve.tensor_tensor(t_lo[:, half * 4:half * 4 + 4, :], ps_t[:, half, :].rearrange("p (c n) -> p c n", n=P),
                                          t_hi[:, half * 4:half * 4 + 4, :].bitcast(F32), ALU.subtract).then_inc(t_lo_done, 1)

        @block.tensor
        def _(pe):
            def mix(b, t, slot_free):
                first_tile = isinstance(b, int) and b == 0 and t == 0
                pe.wait_ge(m_in[t], past((b + 1) * 32))
                pe.wait_ge(added, past(slot_free * 2))
                for kc in range(KC):
                    if first_tile:
                        pe.wait_ge(lo_done, past(kc + 1))
                    for half in range(2):
                        cols = slice(half * HALF, (half + 1) * HALF)
                        mm = three_pass(pe, ps_m[:, t % 2, half, :], (m_hi[:, t, kc, :], m_lo[:, t, kc, :]),
                                        (w_hi[:, kc, cols], w_lo[:, kc, cols]), kc == 0, kc == KC - 1)
                mm.then_inc(mix_done, 1)

            def turn(b, t):
                n = b * TPB + t
                pe.wait_ge(ln_step, past((n + 1) * STEP))
                for half in range(2):
                    pe.wait_ge(t_lo_done, past(n * 2))
                    for i in range(4):
                        kc = half * 4 + i
                        mm = pe.transpose(ps_t[:, half, i * P:(i + 1) * P], y[:, t, kc * P:(kc + 1) * P], ident[:])
                    mm.then_inc(tr_done, 1)

            mix(0, 0, 0)
            pe.wait_ge(consts_in, past(48))

            def body(b, last):
                for t in range(TPB):
                    if t + 1 < TPB:
                        mix(b, t + 1, b * TPB + t)
                    elif not last:
                        mix(b + 1, 0, b * TPB + t)
                    turn(b, t)
            by_blocks(pe, NBLK, body)


S_BLK = T_SAMPLE // BLK
PAIRS = FC // 2
DN = 2 * FC
EDGE = 2


def by_pairs(eng, body):
    for i in range(2):
        body(i, i, FIRST)
    with eng.Fori(1, PAIRS - 1) as p:
        for i in range(2):
            body(p * 2 + i, i, MIDDLE)
    for i in range(2):
        body(FC - 2 + i, i, LAST)


FIRST, MIDDLE, LAST = range(3)


def mlp(nc, x1, x1t_hi, x1t_lo, w_up, conv, w_down, ln_g, ln_b, y_all):
    with ExitStack() as ctx:
        st = Store(nc, ctx, "mlp")
        gain, shift = st.sb("gain", [P, D]), st.sb("shift", [P, D])
        cw = st.sb("cw", [P, FC, 2, 4])
        xt_hi, xt_lo = st.sb("xt_hi", [P, KC, BLK], F32R), st.sb("xt_lo", [P, KC, BLK], F32R)
        wu_raw = st.sb("wu_raw", [P, 2, KC, 2 * P])
        wu_hi, wu_lo = st.sb("wu_hi", [P, 2, KC, 2 * P], F32R), st.sb("wu_lo", [P, 2, KC, 2 * P], F32R)
        hb = st.sb("hb", [P, 2, 2, BLK + EDGE])
        carry = st.sb("carry", [P, FC, 2, EDGE])
        ta, tg = st.sb("ta", [P, BLK]), st.sb("tg", [P, BLK])
        g = st.sb("g", [P, FC, BLK])
        wd_raw = st.sb("wd_raw", [P, 2, HALF])
        wd_hi, wd_lo = st.sb("wd_hi", [P, 2, HALF], F32R), st.sb("wd_lo", [P, 2, HALF], F32R)
        gk_hi, gk_lo = st.sb("gk_hi", [P, 2, BLK], F32R), st.sb("gk_lo", [P, 2, BLK], F32R)
        y = st.sb("y", [P, TPB, D])
        stats, agg = st.sb("stats", [P, TPB, 2, 6]), st.sb("agg", [P, TPB, 2])
        std, rstd, eps = st.sb("std", [P, TPB]), st.sb("rstd", [P, TPB]), st.sb("eps", [P, 1])
        last_t = st.sb("last_t", [P, 2, FC, 2])
        last_g = st.sb("last_g", [P, FC])
        acc = st.sb("acc", [P, 2, HALF])
        ones = st.sb("ones", [P, 1])
        y_last = st.sb("y_last", [1, D])
        ps_h = st.ps("ps_h", [P, 2, 2, BLK])
        ps_f = st.ps("ps_f", [P, TPB, HALF])

        consts_in, carry_set, consts_set = st.sem("consts_in"), st.sem("carry_set"), st.sem("consts_set")
        xt_in, y_in = st.pool_dma_sem("xt_in"), st.sem("y_in")
        wu_in = [st.sem(f"wu_in_{i}") for i in range(2)]
        wu_first_in = [st.pool_dma_sem(f"wu_first_in_{i}") for i in range(2)]
        wd_in = [st.sem(f"wd_in_{i}") for i in range(2)]
        wu_hi_done, wu_lo_done = st.sem("wu_hi_done"), st.sem("wu_lo_done")
        h_done, h_copied = st.sem("h_done"), st.sem("h_copied")
        edge_set, edge_saved = st.sem("edge_set"), st.sem("edge_saved")
        conv_step, silu_done = st.sem("conv_step"), st.sem("silu_done")
        gk_hi_done, wd_hi_done, dn_lo_done = st.sem("gk_hi_done"), st.sem("wd_hi_done"), st.sem("dn_lo_done")
        f_done, added = st.sem("f_done"), st.sem("added")
        stats_done, var_done, std_done, rstd_done = (st.sem(n) for n in ("stats_done", "var_done", "std_done", "rstd_done"))
        centred, gained = st.sem("centred"), st.sem("gained")
        y_stored, y_free = st.pool_dma_sem("y_stored"), st.sem("y_free")
        last_step, last_silu, acc_step = st.sem("last_step"), st.sem("last_silu"), st.sem("acc_step")
        last_sum, y_last_in, last_stored = st.sem("last_sum"), st.sem("y_last_in"), st.pool_dma_sem("last_stored")
        CONV = 7
        st.start()
        block = ctx.enter_context(nc.Block())

        def rows(b, prompt, t=0, n=TPB):
            return slice(t * P, (t + n) * P) if prompt else bass.ds(T_PROMPT - 1 + b * BLK + t * P, n * P)

        def slot_free(eng, sem, done, c, each=1):
            hold(eng, sem, past((done + c - 1) * each if not isinstance(c, int) or c >= 2 else done * each))

        def load_up(eng, c, i, landed):
            src = w_up[bass.ds(c, 1)].rearrange("o p c n -> p (o c) n")
            eng.dma_start(wu_raw[:, i], src).then_inc(landed[i], 16)

        @block.sync
        def _(sp):
            sp.dma_start(gain[:], ln_g.partition_broadcast(P)).then_inc(consts_in, 16)
            sp.dma_start(shift[:], ln_b.partition_broadcast(P)).then_inc(consts_in, 16)
            sp.dma_start(cw[:], conv).then_inc(consts_in, 16)

            def body(b, prompt):
                def up(c, i, place):
                    if place != FIRST:
                        slot_free(sp, wu_lo_done, b * FC, c)
                        load_up(sp, c, i, wu_in)
                by_pairs(sp, up)
                hold(sp, y_free, past(b))
                sp.dma_start(y[:], x1[rows(b, prompt), :].rearrange("(t p) d -> p t d", p=P)).then_inc(y_in, 16)
                if prompt:
                    sp.dma_start(y_last[:], x1[TOK - 1:TOK, :]).then_inc(y_last_in, 16)
                for half in range(2):
                    def down(k, i, place):
                        n = k + half * FC
                        slot_free(sp, dn_lo_done, b * DN, n, 2)
                        if prompt:
                            slot_free(sp, acc_step, 0, n)
                        src = w_down[half, bass.ds(k, 1)].rearrange("o p n -> p (o n)")
                        sp.dma_start(wd_raw[:, i], src).then_inc(wd_in[i], 16)
                    by_pairs(sp, down)

            with sp.Fori(0, S_BLK) as b:
                body(b, False)
            body(S_BLK, True)

        @block.gpsimd
        def _(pool):
            def load_block(b, prompt):
                hold(pool, h_done, past(b * FC))
                cols = slice(0, BLK) if prompt else bass.ds(T_PROMPT + b * BLK, BLK)
                for src, dst in ((x1t_hi, xt_hi), (x1t_lo, xt_lo)):
                    pool.dma_start(dst[:].bitcast(F32), src[:, cols].rearrange("(c p) n -> p c n", p=P)
                                   ).then_inc(xt_in, 16)
                hold(pool, wu_lo_done, past(b * FC))
                for i in range(2):
                    load_up(pool, i, i, wu_first_in)

            def finish(b, prompt):
                for t in range(TPB):
                    hold(pool, centred, past(b * TPB + t + 1))
                    pool.tensor_tensor(y[:, t, :], y[:, t, :], gain[:], ALU.mult).then_inc(gained, 1)
                    hold(pool, gained, past((b * TPB + t) * 2 + 1))
                    pool.tensor_tensor(y[:, t, :], y[:, t, :], shift[:], ALU.add).then_inc(gained, 1)
                    hold(pool, gained, past((b * TPB + t) * 2 + 2))
                    pool.dma_start(y_all[rows(b, prompt, t, 1), :], y[:, t, :]).then_inc(y_stored, 16)

            load_block(0, False)
            pool.memset(carry[:], 0.0).then_inc(carry_set, 1)
            hold(pool, carry_set, past(1))
            hold(pool, consts_in, past(48))

            def body(b, last):
                def edges(c, i, place):
                    edge = carry[:, bass.ds(c, 1)].rearrange("p o s e -> p (o s) e")
                    slot_free(pool, conv_step, b * FC, c, CONV)
                    hold(pool, edge_saved, past(b * FC))
                    pool.tensor_copy(hb[:, i, :, 0:EDGE], edge).then_inc(edge_set, 1)
                    hold(pool, h_copied, past(b * FC + c + 1))
                    hold(pool, edge_set, past(b * FC + c + 1))
                    pool.tensor_copy(edge, hb[:, i, :, BLK:BLK + EDGE]).then_inc(edge_saved, 1)
                by_pairs(pool, edges)
                load_block(b + 1, last)
                finish(b, False)
                hold(pool, y_stored, (b + 1) * TPB * 16)
                pool.sem_inc(y_free, 1)
            by_blocks(pool, S_BLK, body)
            hold(pool, conv_step, past(S_BLK * FC * CONV))
            for i in range(2):
                for at in (0, BLK + EDGE - 1):
                    pool.memset(hb[:, i, :, at:at + 1], 0.0).then_inc(edge_set, 1)
            hold(pool, y_stored, S_BLK * TPB * 16)
            finish(S_BLK, True)
            n = (S_BLK + 1) * TPB
            hold(pool, centred, past(n + 1))
            pool.tensor_tensor(y_last[:], y_last[:], gain[0:1, :], ALU.mult).then_inc(gained, 1)
            hold(pool, gained, past(n * 2 + 1))
            pool.tensor_tensor(y_last[:], y_last[:], shift[0:1, :], ALU.add).then_inc(gained, 1)
            hold(pool, gained, past(n * 2 + 2))
            pool.dma_start(y_all[TOK - 1:TOK, :], y_last[:]).then_inc(last_stored, 16)
            hold(pool, y_stored, n * 16)
            hold(pool, last_stored, 16)

        @block.scalar
        def _(act):
            def split_up(b, c, i):
                if isinstance(c, int) and c < 2:
                    act.wait_ge(wu_first_in[i], (b + 1) * 16)
                else:
                    act.wait_ge(wu_in[i], past((b * (FC - 2) + c - i) * 8))
                slot_free(act, h_done, b * FC, c)
                act.activation(wu_hi[:, i], wu_raw[:, i], ACT.Copy).then_inc(wu_hi_done, 1)

            def split_down(b, n, k, i):
                act.wait_ge(conv_step, past((b * FC + k + 1) * CONV))
                act.wait_ge(wd_in[i], past((b * DN + n - i) * 8 + 16))
                slot_free(act, f_done, b * DN, n)
                act.activation(gk_hi[:, i, :], g[:, bass.ds(k, 1), :].rearrange("p o n -> p (o n)"), ACT.Copy
                               ).then_inc(gk_hi_done, 1)
                act.activation(wd_hi[:, i, :], wd_raw[:, i, :], ACT.Copy).then_inc(wd_hi_done, 1)

            def body(b, prompt):
                if prompt:
                    act.wait_ge(last_step, past(4))
                    act.activation(last_t[:, 1, :, 0], last_t[:, 0, :, 1], ACT.Silu).then_inc(last_silu, 1)

                def up(c, i, place):
                    act.wait_ge(h_done, past(b * FC + c + 1))
                    slot_free(act, conv_step, b * FC, c, CONV)
                    if not prompt:
                        slot_free(act, edge_saved, b * FC, c)
                    at = 1 if prompt else EDGE
                    act.activation(hb[:, i, :, at:at + BLK], ps_h[:, i], ACT.Copy).then_inc(h_copied, 1)
                    if place == LAST:
                        split_down(b, i, i, i)
                    else:
                        split_up(b, c + 2, i)
                    act.wait_ge(conv_step, past((b * FC + c) * CONV + 3))
                    act.activation(tg[:], tg[:], ACT.Silu).then_inc(silu_done, 1)
                by_pairs(act, up)
                for half in range(2):
                    def down(k, i, place):
                        if place != LAST:
                            split_down(b, k + 2 + half * FC, k + 2, i)
                        elif half == 0:
                            split_down(b, FC + i, i, i)
                        elif not prompt:
                            split_up(b + 1, i, i)
                    by_pairs(act, down)
                act.wait_ge(var_done, past(b + 1))
                act.activation(std[:], agg[:, :, 1], ACT.Sqrt, bias=eps[:, 0:1]).then_inc(std_done, 1)

            act.wait_ge(consts_set, past(3))
            for i in range(2):
                split_up(0, i, i)
            with act.Fori(0, S_BLK) as b:
                body(b, False)
            body(S_BLK, True)
            act.wait_ge(var_done, past(S_BLK + 2))
            act.activation(std[0:1, 0:1], agg[0:1, 0, 1:2], ACT.Sqrt, bias=eps[0:1, 0:1]).then_inc(std_done, 1)

        @block.vector
        def _(dve):
            def split_up(b, c, i):
                dve.wait_ge(wu_hi_done, past(b * FC + c + 1))
                dve.tensor_tensor(wu_lo[:, i], wu_raw[:, i], wu_hi[:, i].bitcast(F32), ALU.subtract).then_inc(wu_lo_done, 1)

            def split_down(b, n, k, i, prompt):
                dve.wait_ge(gk_hi_done, past(b * DN + n + 1))
                dve.tensor_tensor(gk_lo[:, i, :], g[:, bass.ds(k, 1), :].rearrange("p o n -> p (o n)"),
                                  gk_hi[:, i, :].bitcast(F32), ALU.subtract).then_inc(dn_lo_done, 1)
                dve.wait_ge(wd_hi_done, past(b * DN + n + 1))
                dve.tensor_tensor(wd_lo[:, i, :], wd_raw[:, i, :], wd_hi[:, i, :].bitcast(F32),
                                  ALU.subtract).then_inc(dn_lo_done, 1)

            def add_last(half, k, i):
                dve.wait_ge(acc_step, past(k + half * FC))
                dve.scalar_tensor_tensor(acc[:, half, :], wd_raw[:, i, :], last_g[:, bass.ds(k, 1)], acc[:, half, :],
                                         ALU.mult, ALU.add).then_inc(acc_step, 1)

            def convolve(b, c, i, out, s, step):
                tap = cw[:, bass.ds(c, 1), s, :].rearrange("p o w -> p (o w)")
                base = (b * FC + c) * CONV + step
                dve.tensor_scalar(out[:], hb[:, i, s, 0:BLK], tap[:, 0:1], tap[:, 3:4], ALU.mult, ALU.add
                                  ).then_inc(conv_step, 1)
                for j in (1, 2):
                    dve.wait_ge(conv_step, past(base + j))
                    dve.scalar_tensor_tensor(out[:], hb[:, i, s, j:j + BLK], tap[:, j:j + 1], out[:], ALU.mult, ALU.add
                                             ).then_inc(conv_step, 1)

            def body(b, prompt):
                if prompt:
                    dve.wait_ge(edge_saved, past(S_BLK * FC))
                    for j in range(2):
                        dve.tensor_tensor(last_t[:, j], carry[:, :, :, j], cw[:, :, :, j], ALU.mult).then_inc(last_step, 1)
                    dve.wait_ge(last_step, past(2))
                    dve.tensor_tensor(last_t[:, 0], last_t[:, 0], last_t[:, 1], ALU.add).then_inc(last_step, 1)
                    dve.wait_ge(last_step, past(3))
                    dve.tensor_tensor(last_t[:, 0], last_t[:, 0], cw[:, :, :, 3], ALU.add).then_inc(last_step, 1)
                    dve.wait_ge(last_silu, past(1))
                    dve.tensor_tensor(last_g[:], last_t[:, 0, :, 0], last_t[:, 1, :, 0], ALU.mult).then_inc(last_step, 1)
                    dve.wait_ge(last_step, past(5))

                def up(c, i, place):
                    dve.wait_ge(h_copied, past(b * FC + c + 1))
                    dve.wait_ge(edge_set, past(S_BLK * FC + 4 if prompt else b * FC + c + 1))
                    dve.wait_ge(conv_step, past((b * FC + c) * CONV))
                    convolve(b, c, i, tg, 1, 0)
                    convolve(b, c, i, ta, 0, 3)
                    if place == LAST:
                        split_down(b, i, i, i, prompt)
                    else:
                        split_up(b, c + 2, i)
                    dve.wait_ge(conv_step, past((b * FC + c) * CONV + 6))
                    dve.wait_ge(silu_done, past(b * FC + c + 1))
                    dve.tensor_tensor(g[:, bass.ds(c, 1), :].rearrange("p o n -> p (o n)"), tg[:], ta[:], ALU.mult
                                      ).then_inc(conv_step, 1)
                by_pairs(dve, up)
                for half in range(2):
                    if half == 0:
                        dve.wait_ge(conv_step, past((b + 1) * FC * CONV))

                    def down(k, i, place):
                        if prompt:
                            add_last(half, k, i)
                        if place != LAST:
                            split_down(b, k + 2 + half * FC, k + 2, i, prompt)
                        elif half == 0:
                            split_down(b, FC + i, i, i, prompt)
                        elif not prompt:
                            split_up(b + 1, i, i)
                    by_pairs(dve, down)
                    if half == 0:
                        dve.wait_ge(y_in, past((b + 1) * 16))
                    dve.wait_ge(f_done, past(b * DN + (half + 1) * FC))
                    for t in range(TPB):
                        part = y[:, t, half * HALF:(half + 1) * HALF]
                        dve.scalar_tensor_tensor(part, part, ALPHA, ps_f[:, t, :], ALU.mult, ALU.add).then_inc(added, 1)
                dve.wait_ge(added, past((b + 1) * 2 * TPB))
                for t in range(TPB):
                    for half in range(2):
                        ins = dve.bn_stats(stats[:, t, half, :], y[:, t, half * HALF:(half + 1) * HALF])
                ins.then_inc(stats_done, 1)
                hold(dve, stats_done, past(b + 1))
                for t in range(TPB):
                    ins = dve.bn_aggr(agg[:, t, :], stats[:, t].rearrange("p h s -> p (h s)"))
                ins.then_inc(var_done, 1)
                dve.wait_ge(std_done, past(b + 1))
                dve.reciprocal(rstd[:], std[:]).then_inc(rstd_done, 1)
                dve.wait_ge(rstd_done, past(b + 1))
                for t in range(TPB):
                    dve.tensor_scalar(y[:, t, :], y[:, t, :], agg[:, t, 0:1], rstd[:, t:t + 1],
                                      ALU.subtract, ALU.mult).then_inc(centred, 1)

            dve.memset(eps[:], LN_EPS).then_inc(consts_set, 1)
            dve.memset(ones[:], 1.0).then_inc(consts_set, 1)
            dve.memset(acc[:], 0.0).then_inc(consts_set, 1)
            dve.wait_ge(consts_set, past(3))
            for i in range(2):
                split_up(0, i, i)
            dve.wait_ge(consts_in, past(48))
            with dve.Fori(0, S_BLK) as b:
                body(b, False)
            body(S_BLK, True)
            dve.wait_ge(y_last_in, past(16))
            dve.wait_ge(last_sum, past(1))
            for half in range(2):
                part = y_last[:, half * HALF:(half + 1) * HALF]
                dve.scalar_tensor_tensor(part, part, ALPHA, ps_h[0:1, 0, half, :], ALU.mult, ALU.add).then_inc(added, 1)
            dve.wait_ge(added, past((S_BLK + 1) * 2 * TPB + 2))
            dve.wait_ge(centred, past((S_BLK + 1) * TPB))
            for half in range(2):
                ins = dve.bn_stats(stats[0:1, 0, half, :], y_last[:, half * HALF:(half + 1) * HALF])
            ins.then_inc(stats_done, 1)
            dve.wait_ge(stats_done, past(S_BLK + 2))
            dve.bn_aggr(agg[0:1, 0, :], stats[0:1, 0].rearrange("p h s -> p (h s)")).then_inc(var_done, 1)
            dve.wait_ge(std_done, past(S_BLK + 2))
            dve.reciprocal(rstd[0:1, 0:1], std[0:1, 0:1]).then_inc(rstd_done, 1)
            dve.wait_ge(rstd_done, past(S_BLK + 2))
            dve.tensor_scalar(y_last[:], y_last[:], agg[0:1, 0, 0:1], rstd[0:1, 0:1],
                              ALU.subtract, ALU.mult).then_inc(centred, 1)

        @block.tensor
        def _(pe):
            def body(b, prompt):
                pe.wait_ge(xt_in, (b + 1) * 32)

                def up(c, i, place):
                    pe.wait_ge(wu_lo_done, past(b * FC + c + 1))
                    slot_free(pe, h_copied, b * FC, c)
                    for s in range(2):
                        cols = slice(s * P, (s + 1) * P)
                        for kc in range(KC):
                            mm = three_pass(pe, ps_h[:, i, s, :], (wu_hi[:, i, kc, cols], wu_lo[:, i, kc, cols]),
                                            (xt_hi[:, kc, :], xt_lo[:, kc, :]), kc == 0, kc == KC - 1)
                    mm.then_inc(h_done, 1)
                by_pairs(pe, up)
                for half in range(2):
                    def down(k, i, place):
                        n = k + half * FC
                        pe.wait_ge(dn_lo_done, past((b * DN + n + 1) * 2))
                        first, last = place == FIRST and i == 0, place == LAST and i == 1
                        for t in range(TPB):
                            if first:
                                pe.wait_ge(added, past(b * 2 * TPB + (t + 1 if half else 0)))
                            cols = slice(t * P, (t + 1) * P)
                            mm = three_pass(pe, ps_f[:, t, :], (gk_hi[:, i, cols], gk_lo[:, i, cols]),
                                            (wd_hi[:, i, :], wd_lo[:, i, :]), first, last)
                        mm.then_inc(f_done, 1)
                    by_pairs(pe, down)

            with pe.Fori(0, S_BLK) as b:
                body(b, False)
            body(S_BLK, True)
            pe.wait_ge(acc_step, past(DN))
            pe.wait_ge(h_copied, past((S_BLK + 1) * FC))
            for half in range(2):
                mm = pe.matmul(ps_h[0:1, 0, half, :], ones[:], acc[:, half, :], start=True, stop=True)
            mm.then_inc(last_sum, 1)


def encoder(nc, a, y_all):
    def scratch(name, *shape):
        return nc.dram_tensor(name, shape, F32).ap()

    xln, x1 = scratch("xln", TOK, D), scratch("x1", TOK, D)
    qk_t, lr_t = scratch("qk_t", 3 * UNITS * P, TOK), scratch("lr_t", 2 * LOWRANK, TOK)
    tok_proj = scratch("tok_proj", 3, TOK, UNITS * P)
    rpb_rep = scratch("rpb_rep", NA_H, ROWS_U, QB_C, BIAS_ROWS * RPB_C)
    mix_hi, mix_lo = scratch("mix_hi", D, TOK), scratch("mix_lo", D, TOK)
    x1t_hi, x1t_lo = scratch("x1t_hi", D, TOK), scratch("x1t_lo", D, TOK)

    project(nc, a["x"], a["ln_in_g"], a["ln_in_b"], a["w_groups"], a["w_lr"], a["ident"], xln, qk_t, lr_t, tok_proj)
    gla(nc, qk_t, lr_t, tok_proj, a["w_gate"], a["b_gate"], a["gla_norm_g"], a["ident"], a["reset"], a["causal"],
        mix_hi, mix_lo)
    natten(nc, qk_t, tok_proj, a["rpb_pad"], a["col_mask"], a["row_mask"], a["ident"], rpb_rep, mix_hi, mix_lo)
    mix_out(nc, xln, mix_hi, mix_lo, a["w_out"], a["ln1_g"], a["ln1_b"], a["ident"], x1, x1t_hi, x1t_lo)
    mlp(nc, x1, x1t_hi, x1t_lo, a["w_up"], a["conv"], a["w_down"], a["ln2_g"], a["ln2_b"], y_all)


def layouts(x_prompt, x_sample, ln_in_g, ln_in_b, w_in, gla_gate_w_fwd, gla_gate_b_fwd, gla_gate_w_bwd,
            gla_gate_b_bwd, gla_norm_g, na_rpb, w_out, ln1_g, ln1_b, w_up, conv_w, conv_b, w_down, ln2_g, ln2_b):
    def packed(v):
        return np.ascontiguousarray(v, dtype=np.float32)

    w = np.asarray(w_in)[0]
    cut = np.cumsum([GLA_H * DK, GLA_H * DK, GLA_H * DV, GLA_H * DV, 2 * LOWRANK, NA_H * DH, NA_H * DH])
    gq, gk, gv, gg, glr, nq, nk, nv = np.split(w, cut, axis=1)
    cols = np.concatenate([gq, gk, nq, nk, gv, gg, nv], axis=1)
    w_lr = np.zeros((D, P), np.float32)
    w_lr[:, :2 * LOWRANK] = glr

    w_gate = np.zeros((GLA_H, 2 * LOWRANK, P), np.float32)
    w_gate[:, :LOWRANK, :DK] = np.asarray(gla_gate_w_fwd)[0].reshape(LOWRANK, GLA_H, DK).transpose(1, 0, 2)
    w_gate[:, LOWRANK:, DK:] = np.asarray(gla_gate_w_bwd)[0].reshape(LOWRANK, GLA_H, DK).transpose(1, 0, 2)
    b_gate = np.concatenate([np.asarray(v)[0].reshape(GLA_H, DK) for v in (gla_gate_b_fwd, gla_gate_b_bwd)], axis=1)

    rpb_pad = np.zeros((NA_H, RPB_R, RPB_C), np.float32)
    rpb_pad[:, PAD_R:PAD_R + 2 * WIN_R - 1, PAD_C:PAD_C + 2 * WIN_C - 1] = np.asarray(na_rpb)[0]
    col_mask, row_mask = natten_masks()

    reset = np.ones((P, TOK), np.float32)
    reset[:, ::CHUNK] = 0.0
    j, i = np.arange(P)[:, None], np.arange(P)[None, :]
    same = j // CHUNK == i // CHUNK
    causal = np.stack([(j <= i) & same, (j >= i) & same], axis=1).astype(np.int32)
    conv = np.concatenate([np.asarray(conv_w)[0], np.asarray(conv_b)], axis=0)
    return {
        "x": packed(np.concatenate([np.asarray(x_prompt)[0], np.asarray(x_sample)[0]])),
        "ln_in_g": packed(ln_in_g), "ln_in_b": packed(ln_in_b),
        "w_groups": packed(cols.reshape(KC, P, GROUPS, UNITS, P).transpose(2, 1, 3, 0, 4)),
        "w_lr": packed(w_lr.reshape(KC, P, P).transpose(1, 0, 2)),
        "w_gate": packed(w_gate), "b_gate": packed(b_gate[:, :, None]), "gla_norm_g": packed(np.asarray(gla_norm_g)[0]),
        "rpb_pad": packed(rpb_pad), "col_mask": col_mask, "row_mask": row_mask,
        "ident": np.eye(P, dtype=np.float32), "reset": reset, "causal": causal,
        "w_out": packed(np.asarray(w_out)[0].reshape(KC, P, D).transpose(1, 0, 2)),
        "ln1_g": packed(np.asarray(ln1_g)[0]), "ln1_b": packed(np.asarray(ln1_b)[0]),
        "w_up": packed(np.asarray(w_up)[0].reshape(KC, P, 2, FC, P).transpose(3, 1, 0, 2, 4)).reshape(FC, P, KC, 2 * P),
        "conv": packed(conv.reshape(4, 2, FC, P).transpose(3, 2, 1, 0)),
        "w_down": packed(np.asarray(w_down)[0].reshape(FC, P, 2, HALF).transpose(2, 0, 1, 3)),
        "ln2_g": packed(np.asarray(ln2_g)[0]), "ln2_b": packed(np.asarray(ln2_b)[0]),
    }


def kernel(**inputs):
    import concourse.bacc as bacc
    from concourse.bass_utils import run_bass_kernel_spmd

    arrays = layouts(**inputs)
    nc = bacc.Bacc("TRN2", target_bir_lowering=False, num_devices=1)
    args = {name: nc.dram_tensor(f"in_{name}", v.shape, mybir.dt.from_np(v.dtype), kind="ExternalInput").ap()
            for name, v in arrays.items()}
    y_all = nc.dram_tensor("y_all", (TOK, D), F32, kind="ExternalOutput").ap()
    encoder(nc, args, y_all)
    run = run_bass_kernel_spmd(nc, [{f"in_{name}": v for name, v in arrays.items()}], core_ids=[0])
    y = run.results[0]["y_all"]
    return y[None, :T_PROMPT], y[None, T_PROMPT:]
```

```python
from contextlib import ExitStack

import concourse.bass as bass
from concourse import mybir
import numpy as np

ALU = mybir.AluOpType
ACT = mybir.ActivationFunctionType
F32 = mybir.dt.float32
F32R = mybir.dt.float32r
I32 = mybir.dt.int32
AX_X = mybir.AxisListType.X

P = 128
D = 1024
KC = D // P
T_PROMPT, T_SAMPLE = 512, 2048
TOK = T_PROMPT + T_SAMPLE
BLK = 512
NBLK = TOK // BLK
TPB = BLK // P
NT = TOK // P

GLA_H, DK, DV, LOWRANK, TAU, CHUNK = 4, 64, 128, 16, 16.0, 64
NCHUNK = TOK // CHUNK
NA_H, DH = 8, 64
GRID_W, WIN_R, WIN_C, QB_C, BAND = 64, 8, 16, 16, 32
D_FF = 2816
FC = D_FF // P
LN_EPS, RMS_EPS = 1e-5, 1e-6
ALPHA = 2.0 ** 0.25
MASKED = -1e30
START = 1

GROUPS = 6
UNITS = 4
T_GROUPS = 3


def by_blocks(eng, n, body):
    with eng.Fori(0, n - 1) as b:
        body(b, False)
    body(n - 1, True)


def past(n):
    return START + n


def hold(eng, sem, value):
    eng.wait_ge(sem, value)
    eng.nop(nofuse=True)


def three_pass(pe, out, lhs, rhs, first, last, skip=False):
    (lh, ll), (rh, rl) = lhs, rhs
    pe.matmul(out, lh, rh, start=first, stop=False, skip_group_check=skip)
    pe.matmul(out, lh, rl, start=False, stop=False, skip_group_check=skip)
    return pe.matmul(out, ll, rh, start=False, stop=last, skip_group_check=skip)


class Store:

    def __init__(self, nc, ctx, stage):
        self.nc, self.ctx, self.stage = nc, ctx, stage
        self.sems = []

    def sb(self, name, shape, dt=F32):
        return self.ctx.enter_context(self.nc.sbuf_tensor(f"{self.stage}_{name}", shape, dt))

    def ps(self, name, shape, dt=F32):
        return self.ctx.enter_context(self.nc.psum_tensor(f"{self.stage}_{name}", shape, dt))

    def sem(self, name):
        self.sems.append(self.ctx.enter_context(self.nc.semaphore(f"{self.stage}_{name}")))
        return self.sems[-1]

    def pool_dma_sem(self, name):
        return self.ctx.enter_context(self.nc.semaphore(f"{self.stage}_{name}"))

    def start(self):
        with self.nc.Block() as block:
            @block.sync
            def _(sp):
                for sem in self.sems:
                    sp.sem_inc(sem, START)


def project(nc, x, ln_g, ln_b, w_groups, w_lr, ident_in, xln, qk_t, lr_t, tok_proj):
    with ExitStack() as ctx:
        st = Store(nc, ctx, "project")
        ident = st.sb("ident", [P, P])
        gain, shift = st.sb("gain", [P, D]), st.sb("shift", [P, D])
        xb = st.sb("xb", [P, TPB, D])
        stats = st.sb("stats", [P, TPB, 2, 6])
        agg = st.sb("agg", [P, TPB, 2])
        std, rstd = st.sb("std", [P, TPB]), st.sb("rstd", [P, TPB])
        eps = st.sb("eps", [P, 1])
        xt_hi, xt_lo = st.sb("xt_hi", [P, KC, BLK], F32R), st.sb("xt_lo", [P, KC, BLK], F32R)
        w_raw = st.sb("w_raw", [P, 2, UNITS, KC, P])
        w_hi, w_lo = (st.sb(f"w_{s}", [P, 2, UNITS, KC, P], F32R) for s in ("hi", "lo"))
        lr_raw = w_raw[:, 1, 0]
        lr_hi, lr_lo = st.sb("lr_hi", [P, KC, P], F32R), st.sb("lr_lo", [P, KC, P], F32R)
        out = st.sb("out", [P, UNITS, BLK])
        out_lr = st.sb("out_lr", [P, BLK])
        ps_t = st.ps("ps_t", [P, 2, BLK])
        ps_o = st.ps("ps_o", [P, UNITS, BLK])
        ps_lr = st.ps("ps_lr", [P, BLK])

        consts_in = st.sem("consts_in")
        x_in = st.sem("x_in")
        x_stored = st.sem("x_stored")
        w_in_slot = [st.sem(f"w_in_{i}") for i in range(2)]
        eps_set = st.sem("eps_set")
        stats_done = st.sem("stats_done")
        std_done = st.sem("std_done")
        ln_step = st.sem("ln_step")
        tr_done = st.sem("tr_done")
        xt_hi_done, xt_lo_done = st.sem("xt_hi_done"), st.sem("xt_lo_done")
        hi_done, lo_done = st.sem("hi_done"), st.sem("lo_done")
        lr_hi_done, lr_lo_done = st.sem("lr_hi_done"), st.sem("lr_lo_done")
        acc_done = st.sem("acc_done")
        lr_done = st.sem("lr_done")
        copied_act, copied_dve = st.sem("copied_act"), st.sem("copied_dve")
        lr_copied = st.sem("lr_copied")
        out_stored = [st.sem(f"out_stored_{u}") for u in range(UNITS)]
        lr_stored = st.sem("lr_stored")
        LN_STEPS = 2 + 3 * TPB
        st.start()
        block = ctx.enter_context(nc.Block())

        def x_rows(b):
            return x[bass.ds(b * BLK, BLK), :].rearrange("(t p) d -> p t d", p=P)

        @block.sync
        def _(sp):
            sp.dma_start(xb[:], x_rows(0)).then_inc(x_in, 16)
            sp.dma_start(gain[:], ln_g.partition_broadcast(P)).then_inc(consts_in, 16)
            sp.dma_start(shift[:], ln_b.partition_broadcast(P)).then_inc(consts_in, 16)
            sp.dma_start(ident[:], ident_in).then_inc(consts_in, 16)
            sp.dma_start(lr_raw, w_lr).then_inc(consts_in, 16)
            sp.dma_start(w_raw[:, 0], w_groups[0]).then_inc(w_in_slot[0], 16)
            hold(sp, lr_lo_done, past(1))

            def load(b, g, last):
                if not (last and g == GROUPS):
                    hold(sp, lo_done, past(b * GROUPS * UNITS + (g - 1) * UNITS))
                    sp.dma_start(w_raw[:, g % 2], w_groups[g % GROUPS]).then_inc(w_in_slot[g % 2], 16)

            def body(b, last):
                hold(sp, ln_step, past((b + 1) * LN_STEPS))
                sp.dma_start(xln[bass.ds(b * BLK, BLK), :].rearrange("(t p) d -> p t d", p=P),
                             xb[:]).then_inc(x_stored, 16)
                load(b, 1, last)
                if not last:
                    hold(sp, x_stored, past((b + 1) * 16))
                    hold(sp, tr_done, past((b + 1) * KC))
                    sp.dma_start(xb[:], x_rows(b + 1)).then_inc(x_in, 16)
                hold(sp, lr_copied, past(b + 1))
                sp.dma_start(lr_t[:, bass.ds(b * BLK, BLK)], out_lr[0:2 * LOWRANK, :]).then_inc(lr_stored, 16)
                for g in range(GROUPS):
                    if g:
                        load(b, g + 1, last)
                    for u in range(UNITS):
                        hold(sp, copied_act if u < 2 else copied_dve, past(b * GROUPS * 2 + g * 2 + u % 2 + 1))
                        if g < T_GROUPS:
                            dst = qk_t[(g * UNITS + u) * P:(g * UNITS + u + 1) * P, bass.ds(b * BLK, BLK)]
                        else:
                            dst = tok_proj[g - T_GROUPS, bass.ds(b * BLK + u * P, P), :]
                        sp.dma_start(dst, out[:, u, :]).then_inc(out_stored[u], 16)
            by_blocks(sp, NBLK, body)
            for sem, n in [(x_stored, NBLK), (lr_stored, NBLK)] + [(s, NBLK * GROUPS) for s in out_stored]:
                hold(sp, sem, past(16 * n))

        @block.scalar
        def _(act):
            def split_hi(n_in_block, b, g, u):
                if u == 0:
                    act.wait_ge(w_in_slot[g % 2], past((b * (GROUPS // 2) + g // 2 + 1) * 16))
                if u == 0:
                    act.wait_ge(acc_done, past(n_in_block))
                act.activation(w_hi[:, g % 2, u], w_raw[:, g % 2, u], ACT.Copy).then_inc(hi_done, 1)

            def sqrt(b):
                act.wait_ge(stats_done, past(b + 1))
                act.activation(std[:], agg[:, :, 1], ACT.Sqrt, bias=eps[:, 0:1]).then_inc(std_done, 1)

            act.wait_ge(eps_set, past(1))
            sqrt(0)
            act.wait_ge(consts_in, past(64))
            act.activation(lr_hi[:], lr_raw, ACT.Copy).then_inc(lr_hi_done, 1)
            for u in range(UNITS):
                act.wait_ge(w_in_slot[0], past(16))
                act.activation(w_hi[:, 0, u], w_raw[:, 0, u], ACT.Copy).then_inc(hi_done, 1)

            def body(b, last):
                for kc in range(KC):
                    act.wait_ge(tr_done, past(b * KC + kc + 1))
                    if kc == 0:
                        act.wait_ge(acc_done, past(b * GROUPS * UNITS))
                    act.activation(xt_hi[:, kc, :], ps_t[:, kc % 2, :], ACT.Copy).then_inc(xt_hi_done, 1)
                for g in range(GROUPS):
                    more = not (last and g == GROUPS - 1)
                    for u in range(UNITS):
                        if u < 2:
                            act.wait_ge(acc_done, past(b * GROUPS * UNITS + g * UNITS + u + 1))
                            act.wait_ge(out_stored[u], past((b * GROUPS + g) * 16))
                            act.activation(out[:, u, :], ps_o[:, u, :], ACT.Copy).then_inc(copied_act, 1)
                        if more:
                            nxt = g + 1
                            split_hi(b * GROUPS * UNITS + g * UNITS, b + nxt // GROUPS, nxt % GROUPS, u)
                    if g == 0:
                        act.wait_ge(lr_done, past(b + 1))
                        act.wait_ge(lr_stored, past(b * 16))
                        act.activation(out_lr[:], ps_lr[:], ACT.Copy).then_inc(lr_copied, 1)
                    if g == 1 and not last:
                        sqrt(b + 1)
            by_blocks(act, NBLK, body)

        @block.vector
        def _(dve):
            def split_lo(b, g, u):
                n = b * GROUPS * UNITS + g * UNITS + u
                dve.wait_ge(hi_done, past(n + 1))
                dve.tensor_tensor(w_lo[:, g % 2, u], w_raw[:, g % 2, u],
                                  w_hi[:, g % 2, u].bitcast(F32), ALU.subtract).then_inc(lo_done, 1)

            def statistics(b):
                dve.wait_ge(x_in, past((b + 1) * 16))
                for t in range(TPB):
                    for h in range(2):
                        ins = dve.bn_stats(stats[:, t, h, :], xb[:, t, h * BLK:(h + 1) * BLK])
                ins.then_inc(ln_step, 1)
                hold(dve, ln_step, past(b * LN_STEPS + 1))
                for t in range(TPB):
                    ins = dve.bn_aggr(agg[:, t, :], stats[:, t].rearrange("p h s -> p (h s)"))
                ins.then_inc(stats_done, 1)

            def normalise(b):
                if isinstance(b, int) and b == 0:
                    dve.wait_ge(consts_in, past(64))
                dve.wait_ge(std_done, past(b + 1))
                dve.reciprocal(rstd[:], std[:]).then_inc(ln_step, 1)
                dve.wait_ge(ln_step, past(b * LN_STEPS + 2))
                for t in range(TPB):
                    dve.tensor_scalar(xb[:, t, :], xb[:, t, :], agg[:, t, 0:1], rstd[:, t:t + 1],
                                      ALU.subtract, ALU.mult).then_inc(ln_step, 1)
                    dve.wait_ge(ln_step, past(b * LN_STEPS + 3 + 3 * t))
                    dve.tensor_tensor(xb[:, t, :], xb[:, t, :], gain[:], ALU.mult).then_inc(ln_step, 1)
                    dve.wait_ge(ln_step, past(b * LN_STEPS + 4 + 3 * t))
                    dve.tensor_tensor(xb[:, t, :], xb[:, t, :], shift[:], ALU.add).then_inc(ln_step, 1)

            dve.memset(eps[:], LN_EPS).then_inc(eps_set, 1)
            statistics(0)
            normalise(0)
            dve.wait_ge(lr_hi_done, past(1))
            dve.tensor_tensor(lr_lo[:], lr_raw, lr_hi[:].bitcast(F32), ALU.subtract).then_inc(lr_lo_done, 1)
            for u in range(UNITS):
                split_lo(0, 0, u)

            def body(b, last):
                for kc in range(KC):
                    dve.wait_ge(xt_hi_done, past(b * KC + kc + 1))
                    dve.tensor_tensor(xt_lo[:, kc, :], ps_t[:, kc % 2, :], xt_hi[:, kc, :].bitcast(F32),
                                      ALU.subtract).then_inc(xt_lo_done, 1)
                for g in range(GROUPS):
                    more = not (last and g == GROUPS - 1)
                    for u in range(UNITS):
                        if u >= 2:
                            dve.wait_ge(acc_done, past(b * GROUPS * UNITS + g * UNITS + u + 1))
                            dve.wait_ge(out_stored[u], past((b * GROUPS + g) * 16))
                            dve.tensor_copy(out[:, u, :], ps_o[:, u, :]).then_inc(copied_dve, 1)
                        if more:
                            nxt = g + 1
                            split_lo(b + nxt // GROUPS, nxt % GROUPS, u)
                    if g == 1 and not last:
                        statistics(b + 1)
                    if g == 2 and not last:
                        normalise(b + 1)
            by_blocks(dve, NBLK, body)

        @block.tensor
        def _(pe):
            def body(b, last):
                pe.wait_ge(ln_step, past((b + 1) * LN_STEPS))
                for kc in range(KC):
                    pe.wait_ge(xt_lo_done, past(b * KC + max(kc - 1, 0) if kc < 2 else b * KC + kc - 1))
                    for t in range(TPB):
                        mm = pe.transpose(ps_t[:, kc % 2, t * P:(t + 1) * P],
                                          xb[:, t, kc * P:(kc + 1) * P], ident[:])
                    mm.then_inc(tr_done, 1)
                pe.wait_ge(xt_lo_done, past((b + 1) * KC))
                pe.wait_ge(lr_lo_done, past(1))
                pe.wait_ge(lr_copied, past(b))
                for kc in range(KC):
                    mm = three_pass(pe, ps_lr[:], (lr_hi[:, kc, :], lr_lo[:, kc, :]),
                                    (xt_hi[:, kc, :], xt_lo[:, kc, :]), kc == 0, kc == KC - 1)
                mm.then_inc(lr_done, 1)
                for g in range(GROUPS):
                    for u in range(UNITS):
                        pe.wait_ge(lo_done, past(b * GROUPS * UNITS + g * UNITS + (u if g < T_GROUPS else UNITS - 1) + 1))
                        pe.wait_ge(copied_act if u < 2 else copied_dve, past(b * GROUPS * 2 + (g - 1) * 2 + u % 2 + 1
                                   if g else b * GROUPS * 2))
                        for kc in range(KC):
                            if g < T_GROUPS:
                                lhs = (w_hi[:, g % 2, u, kc, :], w_lo[:, g % 2, u, kc, :])
                                rhs = (xt_hi[:, kc, :], xt_lo[:, kc, :])
                            else:
                                lhs = (xt_hi[:, kc, u * P:(u + 1) * P], xt_lo[:, kc, u * P:(u + 1) * P])
                                rhs = (w_hi[:, g % 2, :, kc, :], w_lo[:, g % 2, :, kc, :])
                            mm = three_pass(pe, ps_o[:, u, :], lhs, rhs, kc == 0, kc == KC - 1)
                        mm.then_inc(acc_done, 1)
            by_blocks(pe, NBLK, body)


GT = 4
NG = NT // GT
SEQS = ((0, T_PROMPT // CHUNK), (T_PROMPT // CHUNK, NCHUNK))


def gla(nc, qk_t, lr_t, tok_proj, w_gate, b_gate, norm_g, ident_in, reset_in, causal_in, mix_hi, mix_lo):
    with ExitStack() as ctx:
        st = Store(nc, ctx, "gla")
        ident = st.sb("ident", [P, P])
        reset = st.sb("reset", [P, TOK])
        causal = st.sb("causal", [P, 2, P], I32)
        gain = st.sb("gain", [P, DV])
        lr = st.sb("lr", [2 * LOWRANK, TOK])
        wg, bg = st.sb("wg", [2 * LOWRANK, P]), st.sb("bg", [P, 1])
        q, k = st.sb("q", [P, TOK]), st.sb("k", [P, TOK])
        v, gate = st.sb("v", [P, NT, DV]), st.sb("gate", [P, NT, DV])
        z, e = st.sb("z", [P, TOK]), st.sb("e", [P, TOK])
        q_in, k_in = st.sb("q_in", [P, TOK]), st.sb("k_in", [P, TOK])
        decay = st.sb("decay", [P, NCHUNK])
        k_tok = st.sb("k_tok", [P, 2, GT, P])
        u = st.sb("u", [P, NCHUNK, DV])
        state = st.sb("state", [P, NCHUNK, DV])
        a_f, a_b = st.sb("a_f", [P, 2, GT, P]), st.sb("a_b", [P, 2, GT, P])
        o = st.sb("o", [P, NT, DV])
        ss, rinv = st.sb("ss", [P, NT]), st.sb("rinv", [P, NT])
        eps = st.sb("eps", [P, 1])
        hi, lo = st.sb("hi", [P, TOK], F32R), st.sb("lo", [P, TOK], F32R)
        ps_w = st.ps("ps_w", [P, 2, BLK])
        ps_k = st.ps("ps_k", [P, BLK])
        ps_u = st.ps("ps_u", [P, 2, BLK])
        ps_f, ps_b = st.ps("ps_f", [P, BLK]), st.ps("ps_b", [P, BLK])
        ps_o = st.ps("ps_o", [P, BLK])

        consts_in, consts_set = st.sem("consts_in"), st.sem("consts_set")
        qk_in, gate_in, wg_in = (st.sem(n) for n in ("qk_in", "gate_in", "wg_in"))
        v_in = [st.sem(f"v_in_{g}") for g in range(NG)]
        z_done, z_copied = st.sem("z_done"), st.sem("z_copied")
        soft_done = st.sem("soft_done")
        la_done, cum_done, rest_done = st.sem("la_done"), st.sem("cum_done"), st.sem("rest_done")
        exp_done = st.sem("exp_done")
        qk_done = st.sem("qk_done")
        kt_done, k_tok_done = st.sem("kt_done"), st.sem("k_tok_done")
        u_done, u_copied = st.sem("u_done"), st.sem("u_copied")
        fwd_step, bwd_step = st.sem("fwd_step"), st.sem("bwd_step")
        a_done, a_masked = st.sem("a_done"), st.sem("a_masked")
        o_done, o_copied = st.sem("o_done"), st.sem("o_copied")
        sq_done, ss_done, ms_done, std_done, rinv_done = (
            st.sem(n) for n in ("sq_done", "ss_done", "ms_done", "std_done", "rinv_done"))
        silu_done, norm_step = st.sem("silu_done"), st.sem("norm_step")
        ot_done, hi_done, lo_done = st.sem("ot_done"), st.sem("hi_done"), st.sem("lo_done")
        stored = st.sem("stored")
        STEPS = sum(b - a - 1 for a, b in SEQS)
        NORM = 2
        gated = st.sem("gated")
        st.start()
        block = ctx.enter_context(nc.Block())

        @block.sync
        def _(sp):
            sp.dma_start(wg[:], w_gate[0]).then_inc(consts_in, 16)
            sp.dma_start(bg[:], b_gate[0]).then_inc(consts_in, 16)
            sp.dma_start(lr[:], lr_t).then_inc(consts_in, 16)
            sp.dma_start(ident[:], ident_in).then_inc(consts_in, 16)
            sp.dma_start(reset[:], reset_in).then_inc(consts_in, 16)
            sp.dma_start(causal[:], causal_in).then_inc(consts_in, 16)
            sp.dma_start(gain[:], norm_g.partition_broadcast(P)).then_inc(consts_in, 16)

            def load_gate_weights(f):
                sp.dma_start(wg[:], w_gate[f]).then_inc(wg_in, 16)
                sp.dma_start(bg[:], b_gate[f]).then_inc(wg_in, 16)

            def load_qk(f):
                for half in range(2):
                    rows = slice(half * DK, (half + 1) * DK)
                    sp.dma_start(k[rows, :], qk_t[bass.ds(GLA_H * DK + f * DK, DK), :]).then_inc(qk_in, 16)
                    sp.dma_start(q[rows, :], qk_t[bass.ds(f * DK, DK), :]).then_inc(qk_in, 16)

            def load_v(f, g):
                rows = slice(g * BLK, (g + 1) * BLK)
                sp.dma_start(v[:, g * GT:(g + 1) * GT, :], tok_proj[0, rows, bass.ds(f * DV, DV)].rearrange(
                    "(t p) d -> p t d", p=P)).then_inc(v_in[g], 16)

            load_qk(0)
            for g in range(NG):
                load_v(0, g)

            def body(h, last):
                if not last:
                    hold(sp, z_copied, past((h + 1) * NBLK))
                    load_gate_weights(h + 1)
                hold(sp, norm_step, past(h * NORM))
                sp.dma_start(gate[:], tok_proj[1, :, bass.ds(h * DV, DV)].rearrange("(t p) d -> p t d", p=P)
                             ).then_inc(gate_in, 16)
                if not last:
                    hold(sp, qk_done, past((h + 1) * 3))
                    load_qk(h + 1)
                    for g in range(NG):
                        hold(sp, o_done, past(h * NG + g + 1))
                        load_v(h + 1, g)
                hold(sp, lo_done, past((h + 1) * NG))
                sp.dma_start(mix_hi[bass.ds(h * DV, DV), :], hi[:].bitcast(F32)).then_inc(stored, 16)
                sp.dma_start(mix_lo[bass.ds(h * DV, DV), :], lo[:].bitcast(F32)).then_inc(stored, 16)
            by_blocks(sp, GLA_H, body)
            hold(sp, stored, past(GLA_H * 32))

        @block.gpsimd
        def _(pool):
            pool.memset(a_f[:], 0.0).then_inc(consts_set, 1)
            pool.memset(a_b[:], 0.0).then_inc(consts_set, 1)
            hold(pool, consts_set, past(7 - len(SEQS)))
            for c0, c1 in SEQS:
                pool.memset(state[DK:P, c1 - 1, :], 0.0).then_inc(consts_set, 1)
            hold(pool, consts_in, past(16 * 7))
            with pool.Fori(0, GLA_H) as h:
                hold(pool, silu_done, past(h + 1))
                wide = gain[:].rearrange("p (a d) -> p a d", a=1).to_broadcast([P, NT, DV])
                pool.tensor_tensor(gate[:], gate[:], wide, ALU.mult).then_inc(gated, 1)

        @block.scalar
        def _(act):
            def softplus(f):
                act.wait_ge(wg_in, past(f * 32))
                act.wait_ge(kt_done, past(f * NG))
                for b in range(NBLK):
                    act.wait_ge(z_done, past(f * NBLK + b + 1))
                    act.activation(z[:, b * BLK:(b + 1) * BLK], ps_w[:, b % 2, :], ACT.Identity,
                                   bias=bg[:, 0:1]).then_inc(z_copied, 1)
                act.wait_ge(z_copied, past((f + 1) * NBLK))
                act.wait_ge(qk_done, past(f * 3))
                act.activation(e[:], z[:], ACT.Abs).then_inc(soft_done, 1)
                act.wait_ge(soft_done, past(f * 3 + 1))
                act.activation(e[:], e[:], ACT.Exp, scale=-1.0).then_inc(soft_done, 1)
                act.wait_ge(soft_done, past(f * 3 + 2))
                act.activation(e[:], e[:], ACT.Ln, bias=1.0).then_inc(soft_done, 1)

            def decays(f):
                act.wait_ge(rest_done, past((f + 1) * 2))
                act.wait_ge(fwd_step, past(f * STEPS))
                act.wait_ge(bwd_step, past(f * STEPS))
                act.activation(decay[0:DK, :], e[0:DK, CHUNK - 1::CHUNK], ACT.Exp, scale=1.0 / TAU)
                act.activation(decay[DK:P, :], e[DK:P, 0::CHUNK], ACT.Exp, scale=1.0 / TAU).then_inc(exp_done, 1)
                act.activation(z[:], z[:], ACT.Exp, scale=1.0 / TAU).then_inc(exp_done, 1)

            def key_factor(f):
                act.wait_ge(ss_done, past(f))
                act.activation(k_in[:], e[:], ACT.Exp, scale=-1.0 / TAU).then_inc(exp_done, 1)

            def query_factor(f):
                act.wait_ge(exp_done, past(f * 4 + 3))
                act.activation(e[:], e[:], ACT.Exp, scale=1.0 / TAU).then_inc(exp_done, 1)

            def copy_keys(f, g):
                act.wait_ge(kt_done, past(f * NG + g + 1))
                if g >= 2:
                    act.wait_ge(u_done, past(f * 2 * NG + 2 * (g - 1)))
                act.activation(k_tok[:, g % 2], ps_k[:], ACT.Copy).then_inc(k_tok_done, 1)

            act.wait_ge(consts_set, past(7))
            softplus(0)
            decays(0)
            key_factor(0)
            query_factor(0)
            for g in range(NG):
                copy_keys(0, g)

            def body(h, last):
                if not last:
                    softplus(h + 1)
                act.wait_ge(gate_in, past((h + 1) * 16))
                act.activation(gate[:], gate[:], ACT.Silu).then_inc(silu_done, 1)
                act.wait_ge(ot_done, past(h * NG))
                for g in range(NG):
                    if g == NG - 1 and not last:
                        decays(h + 1)
                    act.wait_ge(o_done, past(h * NG + g + 1))
                    act.activation(o[:, g * GT:(g + 1) * GT, :], ps_o[:], ACT.Copy).then_inc(o_copied, 1)
                act.wait_ge(o_copied, past((h + 1) * NG))
                act.activation(k_in[:], o[:].rearrange("p t d -> p (t d)"), ACT.Square).then_inc(sq_done, 1)
                if not last:
                    copy_keys(h + 1, 0)
                act.wait_ge(ss_done, past(h + 1))
                act.activation(rinv[:], ss[:], ACT.Sqrt, scale=1.0 / DV, bias=eps[:, 0:1]).then_inc(std_done, 1)
                if not last:
                    copy_keys(h + 1, 1)
                    key_factor(h + 1)
                    copy_keys(h + 1, 2)
                    query_factor(h + 1)
                    copy_keys(h + 1, 3)
                    copy_keys(h + 1, 4)
                act.wait_ge(stored, past(h * 32))
                for g in range(NG):
                    act.wait_ge(ot_done, past(h * NG + g + 1))
                    act.activation(hi[:, g * BLK:(g + 1) * BLK], ps_w[:, g % 2, :], ACT.Copy).then_inc(hi_done, 1)
            by_blocks(act, GLA_H, body)

        @block.vector
        def _(dve):
            def log_decay(f):
                dve.wait_ge(soft_done, past((f + 1) * 3))
                dve.scalar_tensor_tensor(z[:], z[:], 0.0, e[:], ALU.min, ALU.subtract).then_inc(la_done, 1)

            def running_sum(f, backward):
                dve.wait_ge(la_done, past(f + 1))
                if backward:
                    dve.tensor_tensor_scan(e[DK:P, ::-1], reset[DK:P, :], z[DK:P, ::-1], 0.0,
                                           ALU.mult, ALU.add).then_inc(cum_done, 1)
                else:
                    dve.tensor_tensor_scan(e[0:DK, :], reset[0:DK, :], z[0:DK, :], 0.0,
                                           ALU.mult, ALU.add).then_inc(cum_done, 1)

            def rest_of_chunk(f):
                dve.wait_ge(cum_done, past((f + 1) * 2))
                for rows, end in ((slice(0, DK), CHUNK - 1), (slice(DK, P), 0)):
                    by_chunk = e[rows, :].rearrange("p (c i) -> p c i", i=CHUNK)
                    whole = by_chunk[:, :, end:end + 1].to_broadcast([DK, NCHUNK, CHUNK])
                    dve.tensor_tensor(z[rows, :].rearrange("p (c i) -> p c i", i=CHUNK), whole, by_chunk,
                                      ALU.subtract).then_inc(rest_done, 1)

            def scale_k_end(f):
                dve.wait_ge(qk_in, past((f + 1) * 64))
                dve.wait_ge(exp_done, past(f * 4 + 2))
                dve.tensor_tensor(z[:], k[:], z[:], ALU.mult).then_inc(qk_done, 1)

            def scale_k_in(f):
                dve.wait_ge(exp_done, past(f * 4 + 3))
                dve.tensor_tensor(k_in[:], k[:], k_in[:], ALU.mult).then_inc(qk_done, 1)

            def scale_q_in(f):
                dve.wait_ge(exp_done, past(f * 4 + 4))
                dve.wait_ge(o_done, past(f * NG))
                dve.scalar_tensor_tensor(q_in[:], q[:], DK ** -0.5, e[:], ALU.mult, ALU.mult).then_inc(qk_done, 1)

            def copy_sums(f, g):
                for half in range(2):
                    dve.wait_ge(u_done, past(f * 2 * NG + 2 * g + half + 1))
                    c = 2 * g * GT
                    dve.tensor_copy(u[:, c + half:c + 2 * GT:2, :],
                                    ps_u[:, half, :].rearrange("p (t d) -> p t d", d=DV)).then_inc(u_copied, 1)

            def mask(h, g):
                if g >= 2:
                    dve.wait_ge(o_done, past(h * NG + g - 1))
                hold(dve, a_done, past(h * NG + g + 1))
                for d, (ps, a) in enumerate(((ps_f, a_f), (ps_b, a_b))):
                    m = causal[:, d:d + 1, :].to_broadcast([P, GT, P])
                    ins = dve.copy_predicated(a[:, g % 2], m, ps[:].rearrange("p (t i) -> p t i", i=P))
                ins.then_inc(a_masked, 1)

            def states(h):
                dve.wait_ge(u_copied, past((h + 1) * 2 * NG))
                dve.wait_ge(exp_done, past(h * 4 + 1))
                dve.wait_ge(o_done, past(h * NG))
                n = 0
                for c0, c1 in SEQS:
                    for j in range(c1 - c0 - 1):
                        for rows, c, to, step in ((slice(0, DK), c0 + j, c0 + j + 1, fwd_step),
                                                  (slice(DK, P), c1 - 1 - j, c1 - 2 - j, bwd_step)):
                            if n:
                                dve.wait_ge(step, past(h * STEPS + n))
                            dve.scalar_tensor_tensor(state[rows, to, :], state[rows, c, :], decay[rows, c:c + 1],
                                                     u[rows, c, :], ALU.mult, ALU.add).then_inc(step, 1)
                        n += 1

            dve.memset(eps[:], RMS_EPS).then_inc(consts_set, 1)
            for c0, c1 in SEQS:
                dve.memset(state[0:DK, c0, :], 0.0).then_inc(consts_set, 1)
            dve.wait_ge(consts_set, past(7))
            dve.wait_ge(consts_in, past(16 * 7))
            log_decay(0)
            for backward in range(2):
                running_sum(0, backward)
            rest_of_chunk(0)
            scale_k_end(0)
            scale_k_in(0)
            scale_q_in(0)
            for g in range(NG):
                copy_sums(0, g)

            def body(h, last):
                mask(h, 0)
                states(h)
                mask(h, 1)
                if not last:
                    log_decay(h + 1)
                mask(h, 2)
                if not last:
                    running_sum(h + 1, 0)
                mask(h, 3)
                if not last:
                    running_sum(h + 1, 1)
                mask(h, 4)
                if not last:
                    rest_of_chunk(h + 1)
                    scale_k_end(h + 1)
                dve.wait_ge(sq_done, past(h + 1))
                dve.tensor_reduce(ss[:], k_in[:].rearrange("p (t d) -> p t d", d=DV), AX_X, ALU.add).then_inc(ss_done, 1)
                if not last:
                    copy_sums(h + 1, 0)
                dve.wait_ge(std_done, past(h + 1))
                dve.reciprocal(rinv[:], rinv[:]).then_inc(rinv_done, 1)
                if not last:
                    copy_sums(h + 1, 1)
                dve.wait_ge(rinv_done, past(h + 1))
                wide = rinv[:].rearrange("p (t a) -> p t a", a=1).to_broadcast([P, NT, DV])
                dve.tensor_tensor(o[:], o[:], wide, ALU.mult).then_inc(norm_step, 1)
                if not last:
                    copy_sums(h + 1, 2)
                dve.wait_ge(norm_step, past(h * NORM + 1))
                dve.wait_ge(gated, past(h + 1))
                dve.tensor_tensor(o[:], o[:], gate[:], ALU.mult).then_inc(norm_step, 1)
                if not last:
                    copy_sums(h + 1, 3)
                    scale_k_in(h + 1)
                    copy_sums(h + 1, 4)
                    scale_q_in(h + 1)
                for g in range(NG):
                    dve.wait_ge(hi_done, past(h * NG + g + 1))
                    dve.tensor_tensor(lo[:, g * BLK:(g + 1) * BLK], ps_w[:, g % 2, :],
                                      hi[:, g * BLK:(g + 1) * BLK].bitcast(F32), ALU.subtract).then_inc(lo_done, 1)
            by_blocks(dve, GLA_H, body)

        @block.tensor
        def _(pe):
            def gate_logits(f, before):
                pe.wait_ge(wg_in, past(f * 32))
                pe.wait_ge(lo_done, past(before * NG))
                for b in range(NBLK):
                    if b >= 2:
                        pe.wait_ge(z_copied, past(f * NBLK + b - 1))
                    pe.matmul(ps_w[:, b % 2, :], wg[:], lr[:, b * BLK:(b + 1) * BLK],
                              start=True, stop=True).then_inc(z_done, 1)

            def keys_by_token(f, g):
                pe.wait_ge(k_tok_done, past(f * NG + g))
                for i in range(GT):
                    t = g * GT + i
                    mm = pe.transpose(ps_k[:, i * P:(i + 1) * P], z[:, t * P:(t + 1) * P], ident[:])
                mm.then_inc(kt_done, 1)

            def chunk_sums(f, g):
                pe.wait_ge(k_tok_done, past(f * NG + g + 1))
                pe.wait_ge(v_in[g], past((f + 1) * 16))
                pe.wait_ge(u_copied, past(f * 2 * NG + 2 * g))
                for i in range(GT):
                    for c in range(2):
                        rows = slice(c * CHUNK, (c + 1) * CHUNK)
                        mm = pe.matmul(ps_u[:, c, i * DV:(i + 1) * DV], k_tok[rows, g % 2, i, :],
                                       v[rows, g * GT + i, :], start=True, stop=True)
                        if i == GT - 1:
                            mm.then_inc(u_done, 1)

            def sums(f):
                pe.wait_ge(qk_done, past(f * 3 + 1))
                keys_by_token(f, 0)
                for g in range(NG):
                    chunk_sums(f, g)
                    if g + 1 < NG:
                        keys_by_token(f, g + 1)

            def scores(h, g):
                pe.wait_ge(a_masked, past(h * NG + g))
                for rows, ps in ((slice(0, DK), ps_f), (slice(DK, P), ps_b)):
                    for i in range(GT):
                        cols = slice((g * GT + i) * P, (g * GT + i + 1) * P)
                        mm = pe.matmul(ps[:, i * P:(i + 1) * P], k_in[rows, cols], q_in[rows, cols],
                                       start=True, stop=True)
                mm.then_inc(a_done, 1)

            def outputs(h, g):
                pe.wait_ge(a_masked, past(h * NG + g + 1))
                pe.wait_ge(o_copied, past(h * NG + g))
                for i in range(GT):
                    t = g * GT + i
                    out = ps_o[:, i * P:(i + 1) * P]
                    pe.matmul(out, a_f[:, g % 2, i, :], v[:, t, :], start=True, stop=False)
                    pe.matmul(out, a_b[:, g % 2, i, :], v[:, t, :], start=False, stop=True)
                    for c in range(2):
                        rows = slice(c * CHUNK, (c + 1) * CHUNK)
                        col = t * P + c * CHUNK
                        mm = pe.matmul(ps_o[rows, i * P:(i + 1) * P], q_in[:, col:col + CHUNK],
                                       state[:, 2 * t + c, :], start=False, stop=True, skip_group_check=True)
                mm.then_inc(o_done, 1)

            pe.wait_ge(consts_in, past(16 * 7))
            gate_logits(0, 0)
            sums(0)

            def body(h, last):
                pe.wait_ge(qk_done, past((h + 1) * 3))
                scores(h, 0)
                if not last:
                    gate_logits(h + 1, h)
                pe.wait_ge(fwd_step, past((h + 1) * STEPS))
                pe.wait_ge(bwd_step, past((h + 1) * STEPS))
                for g in range(NG):
                    if g + 1 < NG:
                        scores(h, g + 1)
                    outputs(h, g)
                if not last:
                    sums(h + 1)
                pe.wait_ge(norm_step, past((h + 1) * NORM))
                pe.wait_ge(z_copied, past((h + 1 if last else h + 2) * NBLK))
                for g in range(NG):
                    pe.wait_ge(lo_done, past(h * NG + g - 1 if g >= 2 else h * NG))
                    for i in range(GT):
                        mm = pe.transpose(ps_w[:, g % 2, i * P:(i + 1) * P], o[:, g * GT + i, :], ident[:])
                    mm.then_inc(ot_done, 1)
            by_blocks(pe, GLA_H, body)


NQB = GRID_W // QB_C
ROWS_U = BLK // GRID_W
KG = P // BAND
NKG = TOK // GRID_W // KG
BAND_AT = (0, 8, 24, 32)
BIAS_ROWS, BIAS_COLS = 16, 48
PAD_R, PAD_C = 4, 16
RPB_R, RPB_C = ROWS_U - 1 + BIAS_ROWS, QB_C - 1 + BIAS_COLS
COL_AT = (16, 8, 8, 0)
COL_TYPE = (0, 1, 1, 2)
UNITS_NA = ((0, 2, 4, 0), (2, 3, 4, 8), (3, 4, 0, 20), (5, 4, 0, 20), (7, 3, 0, 36))
TABLE_ROWS = 48
NU = len(UNITS_NA)


def natten_masks():
    a, c = np.divmod(np.arange(P), QB_C)
    col = np.full((P, 3, BAND), MASKED, np.float32)
    kc = np.arange(BAND)[None, :]
    for t, start in enumerate((np.maximum(c - 8, 0), c, np.minimum(c + 8, 16))):
        col[:, t][(kc >= start[:, None]) & (kc < start[:, None] + WIN_C)] = 0.0
    row = np.full((P, TABLE_ROWS), MASKED, np.float32)
    for at, e0, n, start in ((0, 4, 8, np.full(P, 4)), (8, 4, 12, np.maximum(a, 4)),
                             (20, 0, 16, a), (36, 0, 12, np.minimum(a, 4))):
        e = e0 + np.arange(n)[None, :]
        row[:, at:at + n][(e >= start[:, None]) & (e < start[:, None] + WIN_R)] = 0.0
    return col, row


def natten(nc, qk_t, tok_proj, rpb_pad, col_mask, row_mask, ident_in, rpb_rep, mix_hi, mix_lo):
    with ExitStack() as ctx:
        st = Store(nc, ctx, "natten")
        ident = st.sb("ident", [P, P])
        cmask, rmask = st.sb("cmask", [P, 3, BAND]), st.sb("rmask", [P, TABLE_ROWS])
        mask = st.sb("mask", [P, 3, TABLE_ROWS, BAND])
        bias = st.sb("bias", [P, BIAS_ROWS, BIAS_COLS])
        table = st.sb("table", [P, 2, 3, TABLE_ROWS, BAND])
        q_raw, k = st.sb("q_raw", [P, TOK]), st.sb("k", [P, TOK])
        q = st.sb("q", [P, NU, NQB, P])
        v = st.sb("v", [P, 2, NKG, NQB, DH])
        s = st.sb("s", [P, NU, NQB, BLK])
        pt = st.sb("pt", [P, NQB, BLK])
        mx, nmx = st.sb("mx", [P, 2 * NU, NQB]), st.sb("nmx", [P, 2 * NU, NQB])
        den, rden = st.sb("den", [P, 2 * NU, NQB]), st.sb("rden", [P, 2 * NU, NQB])
        hi, lo = st.sb("hi", [P, TOK], F32R), st.sb("lo", [P, TOK], F32R)
        ps_s = st.ps("ps_s", [P, NQB, BLK])
        ps_t = st.ps("ps_t", [P, 2, BLK])
        ps_o = st.ps("ps_o", [P, 2, BLK])

        consts_in, mask_set = st.sem("consts_in"), st.sem("mask_set")
        rep_done = st.sem("rep_done")
        bias_in, table_done = st.sem("bias_in"), st.sem("table_done")
        q_in, k_in, v_in, stored = ([st.sem(f"{n}_{side}") for side in range(2)]
                                    for n in ("q_in", "k_in", "v_in", "stored"))
        q_set = st.sem("q_set")
        s_done, biased, nmx_done = st.sem("s_done"), st.sem("biased"), st.sem("nmx_done")
        exp_done, rden_done, p_done = st.sem("exp_done"), st.sem("rden_done"), st.sem("p_done")
        t_done = st.sem("t_done")
        pt_act, pt_dve = st.sem("pt_act"), st.sem("pt_dve")
        o_done, hi_done, lo_done = (st.sem(n) for n in ("o_done", "hi_done", "lo_done"))
        SC = NU * NQB
        TABLES = 12
        PAIRS = NA_H // 2
        NU2 = 2 * NU
        st.start()
        block = ctx.enter_context(nc.Block())

        def half_of(side):
            return slice(side * DH, (side + 1) * DH)

        @block.sync
        def _(sp):
            def load_bias(h):
                for a in range(ROWS_U):
                    base = rpb_rep[bass.ds(h, 1), a]
                    src = bass.AP(tensor=base.tensor, offset=base.offset + QB_C - 1,
                                  ap=[[BIAS_ROWS * RPB_C - 1, QB_C], [RPB_C, BIAS_ROWS], [1, BIAS_COLS]])
                    sp.dma_start(bias[a * QB_C:(a + 1) * QB_C], src).then_inc(bias_in, 16)

            def load_q(h, side):
                sp.dma_start(q_raw[half_of(side), :], qk_t[bass.ds(4 * P + h * DH, DH), :]).then_inc(q_in[side], 16)

            def load_k(h, side):
                sp.dma_start(k[half_of(side), :], qk_t[bass.ds(8 * P + h * DH, DH), :]).then_inc(k_in[side], 16)

            def load_v(h, side):
                by_row = tok_proj[2, :, bass.ds(h * DH, DH)].rearrange("(g a c) d -> a c g d", a=KG, c=GRID_W)
                for cb in range(NQB):
                    for a in range(KG):
                        sp.dma_start(v[a * BAND:(a + 1) * BAND, side, :, cb, :],
                                     by_row[a, BAND_AT[cb]:BAND_AT[cb] + BAND]).then_inc(v_in[side], 16)

            sp.dma_start(rmask[:], row_mask).then_inc(consts_in, 16)
            sp.dma_start(cmask[:], col_mask).then_inc(consts_in, 16)
            for a in range(ROWS_U):
                src = rpb_pad[:, ROWS_U - 1 - a:ROWS_U - 1 - a + BIAS_ROWS, :].rearrange("h (o r) x -> h o (r x)", o=1)
                sp.dma_start(rpb_rep[:, a], src.to_broadcast([NA_H, QB_C, BIAS_ROWS * RPB_C])).then_inc(rep_done, 16)
            load_q(0, 0)
            load_k(0, 0)
            sp.dma_start(ident[:], ident_in).then_inc(consts_in, 16)
            hold(sp, rep_done, past(16 * ROWS_U))
            load_bias(0)
            load_v(0, 0)

            def body(pair, last):
                for side in range(2):
                    h = pair * 2 + side
                    if not (last and side):
                        hold(sp, table_done, past((h + 1) * TABLES))
                        load_bias(h + 1)
                        hold(sp, q_set, past(h))
                        load_q(h + 1, 1 - side)
                        hold(sp, s_done, past(h * SC))
                        load_k(h + 1, 1 - side)
                        hold(sp, o_done, past(h * NU))
                        load_v(h + 1, 1 - side)
                    hold(sp, lo_done, past((h + 1) * NU))
                    rows = bass.ds(4 * P + h * DH, DH)
                    sp.dma_start(mix_hi[rows, :], hi[half_of(side), :].bitcast(F32)).then_inc(stored[side], 16)
                    sp.dma_start(mix_lo[rows, :], lo[half_of(side), :].bitcast(F32)).then_inc(stored[side], 16)
            by_blocks(sp, PAIRS, body)
            for side in range(2):
                hold(sp, stored[side], past(PAIRS * 32))

        @block.gpsimd
        def _(pool):
            hold(pool, consts_in, past(48))
            for t in range(3):
                pool.tensor_tensor(mask[:, t], rmask[:].rearrange("p (r a) -> p r a", a=1).to_broadcast([P, TABLE_ROWS, BAND]),
                                   cmask[:, t:t + 1, :].to_broadcast([P, TABLE_ROWS, BAND]), ALU.add).then_inc(mask_set, 1)
            hold(pool, mask_set, past(3))

            def tables(h, side):
                hold(pool, bias_in, past((h + 1) * 16 * ROWS_U))
                for t, x in enumerate((16, 8, 0)):
                    for at, e0, n in ((0, 4, 8), (8, 4, 12), (20, 0, 16), (36, 0, 12)):
                        pool.tensor_tensor(table[:, side, t, at:at + n, :], bias[:, e0:e0 + n, x:x + BAND],
                                           mask[:, t, at:at + n, :], ALU.add).then_inc(table_done, 1)

            tables(0, 0)
            tables(1, 1)
            with pool.Fori(0, PAIRS - 1) as pair:
                for side in range(2):
                    h = pair * 2 + side
                    hold(pool, biased, past((h + 1) * SC))
                    tables(h + 2, side)

        @block.scalar
        def _(act):
            def set_queries(h, pair, side):
                rows = half_of(side)
                act.wait_ge(q_in[side], past((pair + 1) * 16))
                for u in range(NU):
                    ins = act.activation(q[rows, u].rearrange("p b (a c) -> p a b c", c=QB_C),
                                         q_raw[rows, u * BLK:(u + 1) * BLK].rearrange("p (a b c) -> p a b c", b=NQB, c=QB_C),
                                         ACT.Copy, scale=DH ** -0.5)
                ins.then_inc(q_set, 1)

            def exps(unit, j, blocks):
                n = UNITS_NA[j % NU][1] * P
                act.wait_ge(nmx_done, past(unit + 1))
                for cb in blocks:
                    act.activation(s[:, j % NU, cb, :n], s[:, j % NU, cb, :n], ACT.Exp, bias=nmx[:, j, cb:cb + 1],
                                   accum_out=den[:, j, cb:cb + 1]).then_inc(exp_done, 1)

            set_queries(0, 0, 0)
            exps(0, 0, range(NQB))

            def body(pair, last):
                for j in range(NU2):
                    unit, side, u = pair * NU2 + j, j // NU, j % NU
                    n = UNITS_NA[u][1] * P
                    for cb in range(0, NQB, 2):
                        act.wait_ge(t_done, past(unit * NQB + cb + 1))
                        act.wait_ge(o_done, past(unit))
                        act.activation(pt[:, cb, :n], ps_t[:, cb % 2, :n], ACT.Copy).then_inc(pt_act, 1)
                        if not (last and j == NU2 - 1):
                            exps(unit + 1, (j + 1) % NU2, (cb, cb + 1))
                    if u == 1 and not (last and side):
                        h = pair * 2 + side
                        act.wait_ge(s_done, past(h * SC))
                        set_queries(h + 1, pair + side, 1 - side)
                    act.wait_ge(o_done, past(unit + 1))
                    if u == 0:
                        act.wait_ge(stored[side], past(pair * 32))
                    rows = half_of(side)
                    act.activation(hi[rows, u * BLK:(u + 1) * BLK].rearrange("p (a b c) -> p b a c", b=NQB, c=QB_C),
                                   ps_o[rows, j % 2, :].rearrange("p (b a c) -> p b a c", b=NQB, c=QB_C),
                                   ACT.Copy).then_inc(hi_done, 1)
            by_blocks(act, PAIRS, body)

        @block.vector
        def _(dve):
            def add_bias(unit, j, cb):
                _, groups, _, at = UNITS_NA[j % NU]
                n, side = groups * P, j // NU
                hold(dve, s_done, past(unit * NQB + cb + 1))
                bias_u = table[:, side, COL_TYPE[cb], at:at + groups * KG, :].rearrange("p r c -> p (r c)")
                dve.tensor_tensor_reduce(s[:, j % NU, cb, :n], ps_s[:, cb, :n], bias_u, 1.0, -3.0e38,
                                         ALU.add, ALU.max, mx[:, j, cb:cb + 1]).then_inc(biased, 1)

            def negate_max(unit, j):
                dve.wait_ge(biased, past((unit + 1) * NQB))
                dve.tensor_scalar(nmx[:, j, :], mx[:, j, :], -1.0, None, ALU.mult).then_inc(nmx_done, 1)

            def normalise(unit, j, cb):
                n = UNITS_NA[j % NU][1] * P
                dve.wait_ge(exp_done, past(unit * NQB + cb + 2))
                dve.reciprocal(rden[:, j, cb:cb + 2], den[:, j, cb:cb + 2]).then_inc(rden_done, 1)
                dve.wait_ge(rden_done, past(unit * 2 + cb // 2 + 1))
                for i in (cb, cb + 1):
                    dve.tensor_scalar(s[:, j % NU, i, :n], s[:, j % NU, i, :n], rden[:, j, i:i + 1], None,
                                      ALU.mult).then_inc(p_done, 1)

            dve.wait_ge(table_done, past(TABLES))
            for unit in range(2):
                for cb in range(NQB):
                    add_bias(unit, unit, cb)
                negate_max(unit, unit)
            for cb in (0, 2):
                normalise(0, 0, cb)

            def body(pair, last):
                for j in range(NU2):
                    unit, side, u = pair * NU2 + j, j // NU, j % NU
                    more, more2 = (not (last and j + ahead >= NU2) for ahead in (1, 2))
                    n = UNITS_NA[u][1] * P
                    if u == NU - 2 and more2:
                        dve.wait_ge(table_done, past((pair * 2 + side + 2) * TABLES))
                    for cb in (1, 3):
                        if cb == 3 and more2:
                            add_bias(unit + 2, (j + 2) % NU2, 1)
                        dve.wait_ge(t_done, past(unit * NQB + cb + 1))
                        dve.wait_ge(o_done, past(unit))
                        dve.tensor_copy(pt[:, cb, :n], ps_t[:, cb % 2, :n]).then_inc(pt_dve, 1)
                        if more2:
                            add_bias(unit + 2, (j + 2) % NU2, cb - 1)
                        if more:
                            normalise(unit + 1, (j + 1) % NU2, cb - 1)
                    if more2:
                        add_bias(unit + 2, (j + 2) % NU2, 3)
                        negate_max(unit + 2, (j + 2) % NU2)
                    dve.wait_ge(hi_done, past(unit + 1))
                    view, rows = "p (a b c) -> p b a c", half_of(side)
                    dve.tensor_tensor(lo[rows, u * BLK:(u + 1) * BLK].rearrange(view, b=NQB, c=QB_C),
                                      ps_o[rows, j % 2, :].rearrange("p (b a c) -> p b a c", b=NQB, c=QB_C),
                                      hi[rows, u * BLK:(u + 1) * BLK].bitcast(F32).rearrange(view, b=NQB, c=QB_C),
                                      ALU.subtract).then_inc(lo_done, 1)
            by_blocks(dve, PAIRS, body)

        @block.tensor
        def _(pe):
            def inputs(pair, side):
                pe.wait_ge(q_set, past(pair * 2 + side + 1))
                pe.wait_ge(k_in[side], past((pair + 1) * 16))

            def scores(unit, j, cb, first_ever=False):
                first, groups, _, _ = UNITS_NA[j % NU]
                side = j // NU
                keys = k[half_of(side), first * KG * GRID_W:(first + groups) * KG * GRID_W]
                keys = keys.rearrange("p (r c) -> p r c", c=GRID_W)
                if not first_ever:
                    pe.wait_ge(biased, past((unit - 1) * NQB + cb + 1))
                pe.matmul(ps_s[:, cb, :groups * P], q[half_of(side), j % NU, cb, :],
                          keys[:, :, BAND_AT[cb]:BAND_AT[cb] + BAND], start=True, stop=True).then_inc(s_done, 1)

            def turn(unit, j, cb):
                groups = UNITS_NA[j % NU][1]
                pe.wait_ge(p_done, past(unit * NQB + cb + 1))
                pe.wait_ge(pt_dve if cb % 2 else pt_act, past(unit * 2 + cb // 2))
                for g in range(groups):
                    mm = pe.transpose(ps_t[:, cb % 2, g * P:(g + 1) * P],
                                      s[:, j % NU, cb, g * P:(g + 1) * P], ident[:])
                mm.then_inc(t_done, 1)

            def weigh_values(unit, j, cb):
                first, groups, _, _ = UNITS_NA[j % NU]
                rows, side = half_of(j // NU), j // NU
                pe.wait_ge(pt_dve if cb % 2 else pt_act, past(unit * 2 + cb // 2 + 1))
                for g in range(groups):
                    mm = pe.matmul(ps_o[rows, j % 2, cb * P:(cb + 1) * P], v[:, side, first + g, cb, :],
                                   pt[:, cb, g * P:(g + 1) * P], start=(g == 0), stop=(g == groups - 1))
                return mm

            inputs(0, 0)
            for unit in range(2):
                for cb in range(NQB):
                    scores(unit, unit, cb, first_ever=unit == 0)
            pe.wait_ge(consts_in, past(48))

            def body(pair, last):
                for j in range(NU2):
                    unit, side, u = pair * NU2 + j, j // NU, j % NU
                    ahead = not (last and j + 2 >= NU2)
                    if u == NU - 2 and ahead:
                        inputs(pair + side, 1 - side)
                    if u == 0:
                        pe.wait_ge(v_in[side], past((pair + 1) * 16 * NQB * KG))
                    turn(unit, j, 0)
                    pe.wait_ge(lo_done, past(unit - 1 if j else unit))
                    for cb in range(NQB):
                        if cb + 1 < NQB:
                            turn(unit, j, cb + 1)
                        if ahead:
                            scores(unit + 2, (j + 2) % NU2, cb)
                        mm = weigh_values(unit, j, cb)
                    mm.then_inc(o_done, 1)
            by_blocks(pe, PAIRS, body)


HALF = D // 2


def mix_out(nc, xln, mix_hi, mix_lo, w_out, ln_g, ln_b, ident_in, x1, x1t_hi, x1t_lo):
    with ExitStack() as ctx:
        st = Store(nc, ctx, "mix_out")
        ident = st.sb("ident", [P, P])
        gain, shift = st.sb("gain", [P, D]), st.sb("shift", [P, D])
        w_raw = st.sb("w_raw", [P, KC, D])
        w_hi, w_lo = st.sb("w_hi", [P, KC, D], F32R), st.sb("w_lo", [P, KC, D], F32R)
        m_hi, m_lo = st.sb("m_hi", [P, TPB, KC, P], F32R), st.sb("m_lo", [P, TPB, KC, P], F32R)
        y = st.sb("y", [P, TPB, D])
        stats, agg = st.sb("stats", [P, 2, 6]), st.sb("agg", [P, 2])
        std, rstd, eps = st.sb("std", [P, 1]), st.sb("rstd", [P, 1]), st.sb("eps", [P, 1])
        t_hi, t_lo = st.sb("t_hi", [P, KC, P], F32R), st.sb("t_lo", [P, KC, P], F32R)
        ps_m = st.ps("ps_m", [P, 2, 2, HALF])
        ps_t = st.ps("ps_t", [P, 2, BLK])

        consts_in, eps_set = st.sem("consts_in"), st.sem("eps_set")
        w_in = [st.sem(f"w_in_{kc}") for kc in range(0, KC, 2)]
        hi_done, lo_done = st.sem("hi_done"), st.sem("lo_done")
        tile_in = [st.sem(f"tile_in_{t}") for t in range(TPB)]
        mix_done, added = st.sem("mix_done"), st.sem("added")
        var_done, std_done, ln_step = st.sem("var_done"), st.sem("std_done"), st.sem("ln_step")
        tr_done, t_hi_done, t_lo_done = st.sem("tr_done"), st.sem("t_hi_done"), st.sem("t_lo_done")
        y_stored = [st.sem(f"y_stored_{t}") for t in range(TPB)]
        t_stored = st.sem("t_stored")
        STEP = 5
        st.start()
        block = ctx.enter_context(nc.Block())

        @block.sync
        def _(sp):

            def load(b, t):
                cols = bass.ds(b * BLK + t * P, P)
                for src, dst in ((mix_hi, m_hi), (mix_lo, m_lo)):
                    sp.dma_start(dst[:, t].bitcast(F32), src[:, cols].rearrange("(c p) n -> p c n", p=P)
                                 ).then_inc(tile_in[t], 16)
                sp.dma_start(y[:, t, :], xln[cols, :]).then_inc(tile_in[t], 16)

            def body(b, last):
                for t in range(TPB):
                    cols = bass.ds(b * BLK + t * P, P)
                    hold(sp, ln_step, past((b * TPB + t + 1) * STEP))
                    sp.dma_start(x1[cols, :], y[:, t, :]).then_inc(y_stored[t], 16)
                    hold(sp, t_lo_done, past((b * TPB + t + 1) * 2))
                    for src, dst in ((t_hi, x1t_hi), (t_lo, x1t_lo)):
                        sp.dma_start(dst[:, cols].rearrange("(c p) n -> p c n", p=P), src[:].bitcast(F32)
                                     ).then_inc(t_stored, 16)
                    if not last:
                        hold(sp, y_stored[t], past((b + 1) * 16))
                        load(b + 1, t)

            for kc in range(0, KC, 2):
                sp.dma_start(w_raw[:, kc:kc + 2], w_out[:, kc:kc + 2]).then_inc(w_in[kc // 2], 16)
                if kc == 0:
                    load(0, 0)
            sp.dma_start(gain[:], ln_g.partition_broadcast(P)).then_inc(consts_in, 16)
            sp.dma_start(shift[:], ln_b.partition_broadcast(P)).then_inc(consts_in, 16)
            sp.dma_start(ident[:], ident_in).then_inc(consts_in, 16)
            for t in range(1, TPB):
                load(0, t)
            by_blocks(sp, NBLK, body)
            for sem in y_stored:
                hold(sp, sem, past(NBLK * 16))
            hold(sp, t_stored, past(NT * 32))

        @block.scalar
        def _(act):
            for kc in range(KC):
                act.wait_ge(w_in[kc // 2], past(16))
                act.activation(w_hi[:, kc], w_raw[:, kc], ACT.Copy).then_inc(hi_done, 1)
            act.wait_ge(eps_set, past(1))

            with act.Fori(0, NBLK) as b:
                for t in range(TPB):
                    n = b * TPB + t
                    act.wait_ge(var_done, past(n + 1))
                    act.activation(std[:], agg[:, 1:2], ACT.Sqrt, bias=eps[:, 0:1]).then_inc(std_done, 1)
                    for half in range(2):
                        act.wait_ge(tr_done, past(n * 2 + half + 1))
                        if half == 0:
                            act.wait_ge(t_stored, past(n * 32))
                        act.activation(t_hi[:, half * 4:half * 4 + 4, :], ps_t[:, half, :], ACT.Copy).then_inc(t_hi_done, 1)

        @block.vector
        def _(dve):
            dve.memset(eps[:], LN_EPS).then_inc(eps_set, 1)
            for kc in range(KC):
                dve.wait_ge(hi_done, past(kc + 1))
                dve.tensor_tensor(w_lo[:, kc], w_raw[:, kc], w_hi[:, kc].bitcast(F32), ALU.subtract).then_inc(lo_done, 1)
            dve.wait_ge(consts_in, past(48))
            with dve.Fori(0, NBLK) as b:
                for t in range(TPB):
                    n = b * TPB + t
                    dve.wait_ge(tile_in[t], past((b + 1) * 48))
                    dve.wait_ge(mix_done, past(n + 1))
                    for half in range(2):
                        cols = slice(half * HALF, (half + 1) * HALF)
                        dve.scalar_tensor_tensor(y[:, t, cols], y[:, t, cols], ALPHA, ps_m[:, t % 2, half, :],
                                                 ALU.mult, ALU.add).then_inc(added, 1)
                    dve.wait_ge(added, past((n + 1) * 2))
                    for half in range(2):
                        ins = dve.bn_stats(stats[:, half, :], y[:, t, half * HALF:(half + 1) * HALF])
                    ins.then_inc(ln_step, 1)
                    hold(dve, ln_step, past(n * STEP + 1))
                    dve.bn_aggr(agg[:], stats[:].rearrange("p h s -> p (h s)")).then_inc(var_done, 1)
                    dve.wait_ge(std_done, past(n + 1))
                    dve.reciprocal(rstd[:], std[:]).then_inc(ln_step, 1)
                    dve.wait_ge(ln_step, past(n * STEP + 2))
                    dve.tensor_scalar(y[:, t, :], y[:, t, :], agg[:, 0:1], rstd[:, 0:1],
                                      ALU.subtract, ALU.mult).then_inc(ln_step, 1)
                    dve.wait_ge(ln_step, past(n * STEP + 3))
                    dve.tensor_tensor(y[:, t, :], y[:, t, :], gain[:], ALU.mult).then_inc(ln_step, 1)
                    dve.wait_ge(ln_step, past(n * STEP + 4))
                    dve.tensor_tensor(y[:, t, :], y[:, t, :], shift[:], ALU.add).then_inc(ln_step, 1)
                    for half in range(2):
                        dve.wait_ge(t_hi_done, past(n * 2 + half + 1))
                        dve.tensor_tensor(t_lo[:, half * 4:half * 4 + 4, :], ps_t[:, half, :].rearrange("p (c n) -> p c n", n=P),
                                          t_hi[:, half * 4:half * 4 + 4, :].bitcast(F32), ALU.subtract).then_inc(t_lo_done, 1)

        @block.tensor
        def _(pe):
            def mix(b, t, slot_free):
                first_tile = isinstance(b, int) and b == 0 and t == 0
                pe.wait_ge(tile_in[t], past((b + 1) * 48))
                pe.wait_ge(added, past(slot_free * 2))
                for kc in range(KC):
                    if first_tile:
                        pe.wait_ge(lo_done, past(kc + 1))
                    for half in range(2):
                        cols = slice(half * HALF, (half + 1) * HALF)
                        mm = three_pass(pe, ps_m[:, t % 2, half, :], (m_hi[:, t, kc, :], m_lo[:, t, kc, :]),
                                        (w_hi[:, kc, cols], w_lo[:, kc, cols]), kc == 0, kc == KC - 1)
                mm.then_inc(mix_done, 1)

            def turn(b, t):
                n = b * TPB + t
                pe.wait_ge(ln_step, past((n + 1) * STEP))
                for half in range(2):
                    pe.wait_ge(t_lo_done, past(n * 2))
                    for i in range(4):
                        kc = half * 4 + i
                        mm = pe.transpose(ps_t[:, half, i * P:(i + 1) * P], y[:, t, kc * P:(kc + 1) * P], ident[:])
                    mm.then_inc(tr_done, 1)

            mix(0, 0, 0)
            pe.wait_ge(consts_in, past(48))

            def body(b, last):
                for t in range(TPB):
                    if t + 1 < TPB:
                        mix(b, t + 1, b * TPB + t)
                    elif not last:
                        mix(b + 1, 0, b * TPB + t)
                    turn(b, t)
            by_blocks(pe, NBLK, body)


S_BLK = T_SAMPLE // BLK
PAIRS = FC // 2
DN = 2 * FC
EDGE = 2


def by_pairs(eng, body):
    for i in range(2):
        body(i, i, FIRST)
    with eng.Fori(1, PAIRS - 1) as p:
        for i in range(2):
            body(p * 2 + i, i, MIDDLE)
    for i in range(2):
        body(FC - 2 + i, i, LAST)


def by_phases(eng, up_phase, down_phase):
    up_phase(0, False)
    with eng.Fori(0, S_BLK - 1) as b:
        down_phase(b, False)
        up_phase(b + 1, False, b)
    down_phase(S_BLK - 1, False)
    up_phase(S_BLK, True, S_BLK - 1)
    down_phase(S_BLK, True)


FIRST, MIDDLE, LAST = range(3)


def mlp(nc, x1, x1t_hi, x1t_lo, w_up, conv, w_down, ln_g, ln_b, y_all):
    with ExitStack() as ctx:
        st = Store(nc, ctx, "mlp")
        gain, shift = st.sb("gain", [P, D]), st.sb("shift", [P, D])
        cw = st.sb("cw", [P, FC, 2, 4])
        xt_hi, xt_lo = st.sb("xt_hi", [P, KC, BLK], F32R), st.sb("xt_lo", [P, KC, BLK], F32R)
        wu_raw = st.sb("wu_raw", [P, 2, KC, 2 * P])
        wu_hi, wu_lo = st.sb("wu_hi", [P, 2, KC, 2 * P], F32R), st.sb("wu_lo", [P, 2, KC, 2 * P], F32R)
        hb = st.sb("hb", [P, 2, 2, BLK + EDGE])
        carry = st.sb("carry", [P, FC, 2, EDGE])
        ta, tg = st.sb("ta", [P, BLK]), st.sb("tg", [P, BLK])
        g = st.sb("g", [P, FC, BLK])
        wd_raw = st.sb("wd_raw", [P, 2, HALF])
        wd_hi, wd_lo = st.sb("wd_hi", [P, 2, HALF], F32R), st.sb("wd_lo", [P, 2, HALF], F32R)
        gk_hi, gk_lo = st.sb("gk_hi", [P, 2, BLK], F32R), st.sb("gk_lo", [P, 2, BLK], F32R)
        y = st.sb("y", [P, TPB, D])
        stats, agg = st.sb("stats", [P, TPB, 2, 6]), st.sb("agg", [P, TPB, 2])
        std, rstd, eps = st.sb("std", [P, TPB]), st.sb("rstd", [P, TPB]), st.sb("eps", [P, 1])
        last_t = st.sb("last_t", [P, 2, FC, 2])
        last_g = st.sb("last_g", [P, FC])
        acc = st.sb("acc", [P, 2, HALF])
        ones = st.sb("ones", [P, 1])
        y_last = st.sb("y_last", [1, D])
        ps_h = st.ps("ps_h", [P, 2, 2, BLK])
        ps_f = st.ps("ps_f", [P, TPB, HALF])

        consts_in, consts_set = st.sem("consts_in"), st.sem("consts_set")
        xt_in, y_in = st.pool_dma_sem("xt_in"), st.sem("y_in")
        wu_in = [st.sem(f"wu_in_{i}") for i in range(2)]
        wu_first_in = [st.pool_dma_sem(f"wu_first_in_{i}") for i in range(2)]
        wd_in = [st.sem(f"wd_in_{i}") for i in range(2)]
        wu_hi_done, wu_lo_done = st.sem("wu_hi_done"), st.sem("wu_lo_done")
        h_done, h_copied = st.sem("h_done"), st.sem("h_copied")
        edge_set, edge_saved = st.sem("edge_set"), st.sem("edge_saved")
        conv_step, silu_done = st.sem("conv_step"), st.sem("silu_done")
        gk_hi_done, wd_hi_done, dn_lo_done = st.sem("gk_hi_done"), st.sem("wd_hi_done"), st.sem("dn_lo_done")
        f_done, added = st.sem("f_done"), st.sem("added")
        stats_done, var_done, std_done, rstd_done = (st.sem(n) for n in ("stats_done", "var_done", "std_done", "rstd_done"))
        centred, gained = st.sem("centred"), st.sem("gained")
        y_stored, y_free = st.pool_dma_sem("y_stored"), st.sem("y_free")
        last_step, last_silu, acc_step = st.sem("last_step"), st.sem("last_silu"), st.sem("acc_step")
        last_sum, y_last_in, last_stored = st.sem("last_sum"), st.sem("y_last_in"), st.pool_dma_sem("last_stored")
        CONV = 7
        st.start()
        block = ctx.enter_context(nc.Block())

        def rows(b, prompt, t=0, n=TPB):
            return slice(t * P, (t + n) * P) if prompt else bass.ds(T_PROMPT - 1 + b * BLK + t * P, n * P)

        def slot_free(eng, sem, done, c, each=1):
            hold(eng, sem, past((done + c - 1) * each if not isinstance(c, int) or c >= 2 else done * each))

        def load_up(eng, c, i, landed):
            src = w_up[bass.ds(c, 1)].rearrange("o p c n -> p (o c) n")
            eng.dma_start(wu_raw[:, i], src).then_inc(landed[i], 16)

        @block.sync
        def _(sp):
            sp.dma_start(gain[:], ln_g.partition_broadcast(P)).then_inc(consts_in, 16)
            sp.dma_start(shift[:], ln_b.partition_broadcast(P)).then_inc(consts_in, 16)
            sp.dma_start(cw[:], conv).then_inc(consts_in, 16)

            def body(b, prompt):
                def up(c, i, place):
                    if place != FIRST:
                        slot_free(sp, wu_lo_done, b * FC, c)
                        load_up(sp, c, i, wu_in)
                by_pairs(sp, up)
                hold(sp, y_free, past(b))
                sp.dma_start(y[:], x1[rows(b, prompt), :].rearrange("(t p) d -> p t d", p=P)).then_inc(y_in, 16)
                if prompt:
                    sp.dma_start(y_last[:], x1[TOK - 1:TOK, :]).then_inc(y_last_in, 16)
                for half in range(2):
                    def down(k, i, place):
                        n = k + half * FC
                        slot_free(sp, dn_lo_done, b * DN, n, 2)
                        if prompt:
                            slot_free(sp, acc_step, 0, n)
                        src = w_down[half, bass.ds(k, 1)].rearrange("o p n -> p (o n)")
                        sp.dma_start(wd_raw[:, i], src).then_inc(wd_in[i], 16)
                    by_pairs(sp, down)

            with sp.Fori(0, S_BLK) as b:
                body(b, False)
            body(S_BLK, True)

        @block.gpsimd
        def _(pool):
            def load_block(b, prompt):
                hold(pool, h_done, past(b * FC))
                cols = slice(0, BLK) if prompt else bass.ds(T_PROMPT + b * BLK, BLK)
                for src, dst in ((x1t_hi, xt_hi), (x1t_lo, xt_lo)):
                    pool.dma_start(dst[:].bitcast(F32), src[:, cols].rearrange("(c p) n -> p c n", p=P)
                                   ).then_inc(xt_in, 16)
                hold(pool, wu_lo_done, past(b * FC))
                for i in range(2):
                    load_up(pool, i, i, wu_first_in)

            def finish(b, prompt):
                for t in range(TPB):
                    hold(pool, centred, past(b * TPB + t + 1))
                    pool.tensor_tensor(y[:, t, :], y[:, t, :], gain[:], ALU.mult).then_inc(gained, 1)
                    hold(pool, gained, past((b * TPB + t) * 2 + 1))
                    pool.tensor_tensor(y[:, t, :], y[:, t, :], shift[:], ALU.add).then_inc(gained, 1)
                    hold(pool, gained, past((b * TPB + t) * 2 + 2))
                    pool.dma_start(y_all[rows(b, prompt, t, 1), :], y[:, t, :]).then_inc(y_stored, 16)

            load_block(0, False)
            pool.memset(carry[:], 0.0).then_inc(consts_set, 1)
            hold(pool, consts_in, past(48))

            def body(b, last):
                load_block(b + 1, last)
                finish(b, False)
                hold(pool, y_stored, (b + 1) * TPB * 16)
                pool.sem_inc(y_free, 1)
            by_blocks(pool, S_BLK, body)
            finish(S_BLK, True)
            n = (S_BLK + 1) * TPB
            hold(pool, centred, past(n + 1))
            pool.tensor_tensor(y_last[:], y_last[:], gain[0:1, :], ALU.mult).then_inc(gained, 1)
            hold(pool, gained, past(n * 2 + 1))
            pool.tensor_tensor(y_last[:], y_last[:], shift[0:1, :], ALU.add).then_inc(gained, 1)
            hold(pool, gained, past(n * 2 + 2))
            pool.dma_start(y_all[TOK - 1:TOK, :], y_last[:]).then_inc(last_stored, 16)
            hold(pool, y_stored, n * 16)
            hold(pool, last_stored, 16)

        @block.scalar
        def _(act):
            def split_up(b, c, i):
                if isinstance(c, int) and c < 2:
                    act.wait_ge(wu_first_in[i], (b + 1) * 16)
                else:
                    act.wait_ge(wu_in[i], past((b * (FC - 2) + c - i) * 8))
                slot_free(act, h_done, b * FC, c)
                act.activation(wu_hi[:, i], wu_raw[:, i], ACT.Copy).then_inc(wu_hi_done, 1)

            def split_down(b, n, k, i):
                act.wait_ge(conv_step, past((b * FC + k + 1) * CONV))
                act.wait_ge(wd_in[i], past((b * DN + n - i) * 8 + 16))
                slot_free(act, f_done, b * DN, n)
                act.activation(gk_hi[:, i, :], g[:, bass.ds(k, 1), :].rearrange("p o n -> p (o n)"), ACT.Copy
                               ).then_inc(gk_hi_done, 1)
                act.activation(wd_hi[:, i, :], wd_raw[:, i, :], ACT.Copy).then_inc(wd_hi_done, 1)

            def root(b):
                act.wait_ge(var_done, past(b + 1))
                act.activation(std[:], agg[:, :, 1], ACT.Sqrt, bias=eps[:, 0:1]).then_inc(std_done, 1)

            def up_phase(b, prompt, before=None):
                if prompt:
                    act.wait_ge(last_step, past(4))
                    act.activation(last_t[:, 1, :, 0], last_t[:, 0, :, 1], ACT.Silu).then_inc(last_silu, 1)

                def up(c, i, place):
                    if place == LAST and i == 1:
                        split_down(b, i, i, i)
                    act.wait_ge(h_done, past(b * FC + c + 1))
                    slot_free(act, conv_step, b * FC, c, CONV)
                    if not prompt:
                        slot_free(act, edge_saved, b * FC, c)
                    at = 1 if prompt else EDGE
                    act.activation(hb[:, i, :, at:at + BLK], ps_h[:, i], ACT.Copy).then_inc(h_copied, 1)
                    if place == LAST and i == 0:
                        split_down(b, i, i, i)
                    elif place != LAST:
                        split_up(b, c + 2, i)
                    act.wait_ge(conv_step, past((b * FC + c) * CONV + 3))
                    act.activation(tg[:], tg[:], ACT.Silu).then_inc(silu_done, 1)
                    if place == FIRST and i == 0 and before is not None:
                        root(before)
                by_pairs(act, up)

            def down_phase(b, prompt):
                for half in range(2):
                    def down(k, i, place):
                        if place != LAST:
                            split_down(b, k + 2 + half * FC, k + 2, i)
                        elif half == 0:
                            split_down(b, FC + i, i, i)
                        elif not prompt:
                            split_up(b + 1, i, i)
                    by_pairs(act, down)

            act.wait_ge(consts_set, past(4))
            for i in range(2):
                split_up(0, i, i)
            by_phases(act, up_phase, down_phase)
            root(S_BLK)
            act.wait_ge(var_done, past(S_BLK + 2))
            act.activation(std[0:1, 0:1], agg[0:1, 0, 1:2], ACT.Sqrt, bias=eps[0:1, 0:1]).then_inc(std_done, 1)

        @block.vector
        def _(dve):
            def split_up(b, c, i):
                dve.wait_ge(wu_hi_done, past(b * FC + c + 1))
                dve.tensor_tensor(wu_lo[:, i], wu_raw[:, i], wu_hi[:, i].bitcast(F32), ALU.subtract).then_inc(wu_lo_done, 1)

            def split_down(b, n, k, i, prompt):
                dve.wait_ge(gk_hi_done, past(b * DN + n + 1))
                dve.tensor_tensor(gk_lo[:, i, :], g[:, bass.ds(k, 1), :].rearrange("p o n -> p (o n)"),
                                  gk_hi[:, i, :].bitcast(F32), ALU.subtract).then_inc(dn_lo_done, 1)
                dve.wait_ge(wd_hi_done, past(b * DN + n + 1))
                dve.tensor_tensor(wd_lo[:, i, :], wd_raw[:, i, :], wd_hi[:, i, :].bitcast(F32),
                                  ALU.subtract).then_inc(dn_lo_done, 1)

            def add_last(half, k, i):
                dve.wait_ge(acc_step, past(k + half * FC))
                dve.scalar_tensor_tensor(acc[:, half, :], wd_raw[:, i, :], last_g[:, bass.ds(k, 1)], acc[:, half, :],
                                         ALU.mult, ALU.add).then_inc(acc_step, 1)

            def convolve(b, c, i, out, s, step):
                tap = cw[:, bass.ds(c, 1), s, :].rearrange("p o w -> p (o w)")
                base = (b * FC + c) * CONV + step
                dve.tensor_scalar(out[:], hb[:, i, s, 0:BLK], tap[:, 0:1], tap[:, 3:4], ALU.mult, ALU.add
                                  ).then_inc(conv_step, 1)
                for j in (1, 2):
                    dve.wait_ge(conv_step, past(base + j))
                    dve.scalar_tensor_tensor(out[:], hb[:, i, s, j:j + BLK], tap[:, j:j + 1], out[:], ALU.mult, ALU.add
                                             ).then_inc(conv_step, 1)

            def statistics(b):
                dve.wait_ge(added, past((b + 1) * 2 * TPB))
                for t in range(TPB):
                    for half in range(2):
                        ins = dve.bn_stats(stats[:, t, half, :], y[:, t, half * HALF:(half + 1) * HALF])
                ins.then_inc(stats_done, 1)
                hold(dve, stats_done, past(b + 1))
                for t in range(TPB):
                    ins = dve.bn_aggr(agg[:, t, :], stats[:, t].rearrange("p h s -> p (h s)"))
                ins.then_inc(var_done, 1)

            def centre(b):
                dve.wait_ge(std_done, past(b + 1))
                dve.reciprocal(rstd[:], std[:]).then_inc(rstd_done, 1)
                dve.wait_ge(rstd_done, past(b + 1))
                for t in range(TPB):
                    dve.tensor_scalar(y[:, t, :], y[:, t, :], agg[:, t, 0:1], rstd[:, t:t + 1],
                                      ALU.subtract, ALU.mult).then_inc(centred, 1)

            def up_phase(b, prompt, before=None):
                if prompt:
                    dve.wait_ge(conv_step, past(S_BLK * FC * CONV))
                    for i in range(2):
                        for at in (0, BLK + EDGE - 1):
                            dve.memset(hb[:, i, :, at:at + 1], 0.0).then_inc(edge_set, 1)
                    dve.wait_ge(edge_saved, past(S_BLK * FC))
                    for j in range(2):
                        dve.tensor_tensor(last_t[:, j], carry[:, :, :, j], cw[:, :, :, j], ALU.mult).then_inc(last_step, 1)
                    dve.wait_ge(last_step, past(2))
                    dve.tensor_tensor(last_t[:, 0], last_t[:, 0], last_t[:, 1], ALU.add).then_inc(last_step, 1)
                    dve.wait_ge(last_step, past(3))
                    dve.tensor_tensor(last_t[:, 0], last_t[:, 0], cw[:, :, :, 3], ALU.add).then_inc(last_step, 1)
                    dve.wait_ge(last_silu, past(1))
                    dve.tensor_tensor(last_g[:], last_t[:, 0, :, 0], last_t[:, 1, :, 0], ALU.mult).then_inc(last_step, 1)
                    dve.wait_ge(last_step, past(5))

                def up(c, i, place):
                    if place == LAST and i == 1:
                        split_down(b, i, i, i, prompt)
                    dve.wait_ge(conv_step, past((b * FC + c) * CONV))
                    if not prompt:
                        edge = carry[:, bass.ds(c, 1)].rearrange("p o s e -> p (o s) e")
                        hold(dve, edge_saved, past(b * FC))
                        dve.tensor_copy(hb[:, i, :, 0:EDGE], edge).then_inc(edge_set, 1)
                    hold(dve, h_copied, past(b * FC + c + 1))
                    hold(dve, edge_set, past(S_BLK * FC + 4 if prompt else b * FC + c + 1))
                    if not prompt:
                        dve.tensor_copy(edge, hb[:, i, :, BLK:BLK + EDGE]).then_inc(edge_saved, 1)
                    convolve(b, c, i, tg, 1, 0)
                    convolve(b, c, i, ta, 0, 3)
                    if place == LAST and i == 0:
                        split_down(b, i, i, i, prompt)
                    elif place != LAST:
                        split_up(b, c + 2, i)
                    dve.wait_ge(conv_step, past((b * FC + c) * CONV + 6))
                    dve.wait_ge(silu_done, past(b * FC + c + 1))
                    dve.tensor_tensor(g[:, bass.ds(c, 1), :].rearrange("p o n -> p (o n)"), tg[:], ta[:], ALU.mult
                                      ).then_inc(conv_step, 1)
                    if place == FIRST and before is not None:
                        (statistics, centre)[i](before)
                by_pairs(dve, up)

            def down_phase(b, prompt):
                for half in range(2):
                    if half == 0:
                        dve.wait_ge(conv_step, past((b + 1) * FC * CONV))

                    def down(k, i, place):
                        if prompt:
                            add_last(half, k, i)
                        if place != LAST:
                            split_down(b, k + 2 + half * FC, k + 2, i, prompt)
                        elif half == 0:
                            split_down(b, FC + i, i, i, prompt)
                        elif not prompt:
                            split_up(b + 1, i, i)
                    by_pairs(dve, down)
                    if half == 0:
                        dve.wait_ge(y_in, past((b + 1) * 16))
                    dve.wait_ge(f_done, past(b * DN + (half + 1) * FC))
                    for t in range(TPB):
                        part = y[:, t, half * HALF:(half + 1) * HALF]
                        dve.scalar_tensor_tensor(part, part, ALPHA, ps_f[:, t, :], ALU.mult, ALU.add).then_inc(added, 1)

            dve.memset(eps[:], LN_EPS).then_inc(consts_set, 1)
            dve.memset(ones[:], 1.0).then_inc(consts_set, 1)
            dve.memset(acc[:], 0.0).then_inc(consts_set, 1)
            dve.wait_ge(consts_set, past(4))
            for i in range(2):
                split_up(0, i, i)
            dve.wait_ge(consts_in, past(48))
            by_phases(dve, up_phase, down_phase)
            statistics(S_BLK)
            centre(S_BLK)
            dve.wait_ge(y_last_in, past(16))
            dve.wait_ge(last_sum, past(1))
            for half in range(2):
                part = y_last[:, half * HALF:(half + 1) * HALF]
                dve.scalar_tensor_tensor(part, part, ALPHA, ps_h[0:1, 0, half, :], ALU.mult, ALU.add).then_inc(added, 1)
            dve.wait_ge(added, past((S_BLK + 1) * 2 * TPB + 2))
            dve.wait_ge(centred, past((S_BLK + 1) * TPB))
            for half in range(2):
                ins = dve.bn_stats(stats[0:1, 0, half, :], y_last[:, half * HALF:(half + 1) * HALF])
            ins.then_inc(stats_done, 1)
            dve.wait_ge(stats_done, past(S_BLK + 2))
            dve.bn_aggr(agg[0:1, 0, :], stats[0:1, 0].rearrange("p h s -> p (h s)")).then_inc(var_done, 1)
            dve.wait_ge(std_done, past(S_BLK + 2))
            dve.reciprocal(rstd[0:1, 0:1], std[0:1, 0:1]).then_inc(rstd_done, 1)
            dve.wait_ge(rstd_done, past(S_BLK + 2))
            dve.tensor_scalar(y_last[:], y_last[:], agg[0:1, 0, 0:1], rstd[0:1, 0:1],
                              ALU.subtract, ALU.mult).then_inc(centred, 1)

        @block.tensor
        def _(pe):
            def body(b, prompt):
                pe.wait_ge(xt_in, (b + 1) * 32)

                def up(c, i, place):
                    pe.wait_ge(wu_lo_done, past(b * FC + c + 1))
                    slot_free(pe, h_copied, b * FC, c)
                    for s in range(2):
                        cols = slice(s * P, (s + 1) * P)
                        for kc in range(KC):
                            mm = three_pass(pe, ps_h[:, i, s, :], (wu_hi[:, i, kc, cols], wu_lo[:, i, kc, cols]),
                                            (xt_hi[:, kc, :], xt_lo[:, kc, :]), kc == 0, kc == KC - 1)
                    mm.then_inc(h_done, 1)
                by_pairs(pe, up)
                for half in range(2):
                    def down(k, i, place):
                        n = k + half * FC
                        pe.wait_ge(dn_lo_done, past((b * DN + n + 1) * 2))
                        first, last = place == FIRST and i == 0, place == LAST and i == 1
                        for t in range(TPB):
                            if first:
                                pe.wait_ge(added, past(b * 2 * TPB + (t + 1 if half else 0)))
                            cols = slice(t * P, (t + 1) * P)
                            mm = three_pass(pe, ps_f[:, t, :], (gk_hi[:, i, cols], gk_lo[:, i, cols]),
                                            (wd_hi[:, i, :], wd_lo[:, i, :]), first, last)
                        mm.then_inc(f_done, 1)
                    by_pairs(pe, down)

            with pe.Fori(0, S_BLK) as b:
                body(b, False)
            body(S_BLK, True)
            pe.wait_ge(acc_step, past(DN))
            pe.wait_ge(h_copied, past((S_BLK + 1) * FC))
            for half in range(2):
                mm = pe.matmul(ps_h[0:1, 0, half, :], ones[:], acc[:, half, :], start=True, stop=True)
            mm.then_inc(last_sum, 1)


def encoder(nc, a, y_all):
    def scratch(name, *shape):
        return nc.dram_tensor(name, shape, F32).ap()

    xln, x1 = scratch("xln", TOK, D), scratch("x1", TOK, D)
    qk_t, lr_t = scratch("qk_t", 3 * UNITS * P, TOK), scratch("lr_t", 2 * LOWRANK, TOK)
    tok_proj = scratch("tok_proj", 3, TOK, UNITS * P)
    rpb_rep = scratch("rpb_rep", NA_H, ROWS_U, QB_C, BIAS_ROWS * RPB_C)
    mix_hi, mix_lo = scratch("mix_hi", D, TOK), scratch("mix_lo", D, TOK)
    x1t_hi, x1t_lo = scratch("x1t_hi", D, TOK), scratch("x1t_lo", D, TOK)

    project(nc, a["x"], a["ln_in_g"], a["ln_in_b"], a["w_groups"], a["w_lr"], a["ident"], xln, qk_t, lr_t, tok_proj)
    gla(nc, qk_t, lr_t, tok_proj, a["w_gate"], a["b_gate"], a["gla_norm_g"], a["ident"], a["reset"], a["causal"],
        mix_hi, mix_lo)
    natten(nc, qk_t, tok_proj, a["rpb_pad"], a["col_mask"], a["row_mask"], a["ident"], rpb_rep, mix_hi, mix_lo)
    mix_out(nc, xln, mix_hi, mix_lo, a["w_out"], a["ln1_g"], a["ln1_b"], a["ident"], x1, x1t_hi, x1t_lo)
    mlp(nc, x1, x1t_hi, x1t_lo, a["w_up"], a["conv"], a["w_down"], a["ln2_g"], a["ln2_b"], y_all)


def layouts(x_prompt, x_sample, ln_in_g, ln_in_b, w_in, gla_gate_w_fwd, gla_gate_b_fwd, gla_gate_w_bwd,
            gla_gate_b_bwd, gla_norm_g, na_rpb, w_out, ln1_g, ln1_b, w_up, conv_w, conv_b, w_down, ln2_g, ln2_b):
    def packed(v):
        return np.ascontiguousarray(v, dtype=np.float32)

    w = np.asarray(w_in)[0]
    cut = np.cumsum([GLA_H * DK, GLA_H * DK, GLA_H * DV, GLA_H * DV, 2 * LOWRANK, NA_H * DH, NA_H * DH])
    gq, gk, gv, gg, glr, nq, nk, nv = np.split(w, cut, axis=1)
    cols = np.concatenate([gq, gk, nq, nk, gv, gg, nv], axis=1)
    w_lr = np.zeros((D, P), np.float32)
    w_lr[:, :2 * LOWRANK] = glr

    w_gate = np.zeros((GLA_H, 2 * LOWRANK, P), np.float32)
    w_gate[:, :LOWRANK, :DK] = np.asarray(gla_gate_w_fwd)[0].reshape(LOWRANK, GLA_H, DK).transpose(1, 0, 2)
    w_gate[:, LOWRANK:, DK:] = np.asarray(gla_gate_w_bwd)[0].reshape(LOWRANK, GLA_H, DK).transpose(1, 0, 2)
    b_gate = np.concatenate([np.asarray(v)[0].reshape(GLA_H, DK) for v in (gla_gate_b_fwd, gla_gate_b_bwd)], axis=1)

    rpb_pad = np.zeros((NA_H, RPB_R, RPB_C), np.float32)
    rpb_pad[:, PAD_R:PAD_R + 2 * WIN_R - 1, PAD_C:PAD_C + 2 * WIN_C - 1] = np.asarray(na_rpb)[0]
    col_mask, row_mask = natten_masks()

    reset = np.ones((P, TOK), np.float32)
    reset[:, ::CHUNK] = 0.0
    j, i = np.arange(P)[:, None], np.arange(P)[None, :]
    same = j // CHUNK == i // CHUNK
    causal = np.stack([(j <= i) & same, (j >= i) & same], axis=1).astype(np.int32)
    conv = np.concatenate([np.asarray(conv_w)[0], np.asarray(conv_b)], axis=0)
    return {
        "x": packed(np.concatenate([np.asarray(x_prompt)[0], np.asarray(x_sample)[0]])),
        "ln_in_g": packed(ln_in_g), "ln_in_b": packed(ln_in_b),
        "w_groups": packed(cols.reshape(KC, P, GROUPS, UNITS, P).transpose(2, 1, 3, 0, 4)),
        "w_lr": packed(w_lr.reshape(KC, P, P).transpose(1, 0, 2)),
        "w_gate": packed(w_gate), "b_gate": packed(b_gate[:, :, None]), "gla_norm_g": packed(np.asarray(gla_norm_g)[0]),
        "rpb_pad": packed(rpb_pad), "col_mask": col_mask, "row_mask": row_mask,
        "ident": np.eye(P, dtype=np.float32), "reset": reset, "causal": causal,
        "w_out": packed(np.asarray(w_out)[0].reshape(KC, P, D).transpose(1, 0, 2)),
        "ln1_g": packed(np.asarray(ln1_g)[0]), "ln1_b": packed(np.asarray(ln1_b)[0]),
        "w_up": packed(np.asarray(w_up)[0].reshape(KC, P, 2, FC, P).transpose(3, 1, 0, 2, 4)).reshape(FC, P, KC, 2 * P),
        "conv": packed(conv.reshape(4, 2, FC, P).transpose(3, 2, 1, 0)),
        "w_down": packed(np.asarray(w_down)[0].reshape(FC, P, 2, HALF).transpose(2, 0, 1, 3)),
        "ln2_g": packed(np.asarray(ln2_g)[0]), "ln2_b": packed(np.asarray(ln2_b)[0]),
    }


def kernel(**inputs):
    import concourse.bacc as bacc
    from concourse.bass_utils import run_bass_kernel_spmd

    arrays = layouts(**inputs)
    nc = bacc.Bacc("TRN2", target_bir_lowering=False, num_devices=1)
    args = {name: nc.dram_tensor(f"in_{name}", v.shape, mybir.dt.from_np(v.dtype), kind="ExternalInput").ap()
            for name, v in arrays.items()}
    y_all = nc.dram_tensor("y_all", (TOK, D), F32, kind="ExternalOutput").ap()
    encoder(nc, args, y_all)
    run = run_bass_kernel_spmd(nc, [{f"in_{name}": v for name, v in arrays.items()}], core_ids=[0])
    y = run.results[0]["y_all"]
    return y[None, :T_PROMPT], y[None, T_PROMPT:]
```
